# Optimizing a Trainium2 kernel written in Bass

```python
import math
import jax, jax.numpy as jnp
from jax import lax
import numpy as np

D_MODEL = 1024
BATCH = 1
SEQ = 1024
DEPTH = 1
DEC_BATCH = 8
DEC_SEQ = 8
PAST_LEN = 8192
PAGE_SIZE = 128

S5_WIDTH = D_MODEL // 2
S5_GROUP = 16
S5_GROUPS = S5_WIDTH // S5_GROUP
S5_STATE = 64
LRU_WIDTH = D_MODEL
LRU_HEADS = 8
LRU_HEAD_DIM = LRU_WIDTH // LRU_HEADS
CONV_WIDTH = 4
LRU_C = 8.0
IN_COLS = S5_WIDTH + 2 * LRU_WIDTH + 2 * D_MODEL
SPLITS = (S5_WIDTH, S5_WIDTH + LRU_WIDTH, S5_WIDTH + 2 * LRU_WIDTH, S5_WIDTH + 2 * LRU_WIDTH + D_MODEL)
PEER_HEADS = 8
N_KEYS = 128
N_EXPERTS = N_KEYS * N_KEYS
PEER_TOPK = 16
KEY_HALF = 128
QUERY_DIM = 2 * KEY_HALF
PEER_BLOCK = 128
PLE_DIM = 256
EPS = 1e-6

kernel_name = "hybrid_s5_rglru_peer_decode_step"

F32 = jnp.float32

def rms_norm(x, g):
    xf = x.astype(F32)
    y = xf * lax.rsqrt(jnp.mean(xf * xf, axis=-1, keepdims=True) + EPS)
    return (y * g.astype(F32)).astype(x.dtype)

def _cplx_combine(e1, e2):
    a1r, a1i, b1r, b1i = e1
    a2r, a2i, b2r, b2i = e2
    ar = a2r * a1r - a2i * a1i
    ai = a2r * a1i + a2i * a1r
    br = a2r * b1r - a2i * b1i + b2r
    bi = a2r * b1i + a2i * b1r + b2i
    return ar, ai, br, bi

def _lin_combine(e1, e2):
    a1, b1 = e1
    a2, b2 = e2
    return a1 * a2, a2 * b1 + b2

def s5_branch(u, h0_re, h0_im, lam_re, lam_im, log_dt, b_re, b_im, c_re, c_im, d_skip, w_glu, b_glu):
    n, l, _ = u.shape
    uf = u.astype(F32).reshape(n, l, S5_GROUPS, S5_GROUP)
    dt = jnp.exp(log_dt.astype(F32))[:, None]
    lr, li = lam_re.astype(F32), lam_im.astype(F32)
    mag = jnp.exp(lr * dt)
    abr, abi = mag * jnp.cos(li * dt), mag * jnp.sin(li * dt)
    den = lr * lr + li * li
    nr, ni = abr - 1.0, abi
    coef_r = (nr * lr + ni * li) / den
    coef_i = (ni * lr - nr * li) / den
    br_, bi_ = b_re.astype(F32), b_im.astype(F32)
    bbr = coef_r[..., None] * br_ - coef_i[..., None] * bi_
    bbi = coef_r[..., None] * bi_ + coef_i[..., None] * br_
    bur = jnp.einsum('nlgc,gpc->nlgp', uf, bbr)
    bui = jnp.einsum('nlgc,gpc->nlgp', uf, bbi)
    h0r, h0i = h0_re.astype(F32), h0_im.astype(F32)
    bur = bur.at[:, 0].add(abr * h0r - abi * h0i)
    bui = bui.at[:, 0].add(abr * h0i + abi * h0r)
    ar = jnp.broadcast_to(abr, bur.shape)
    ai = jnp.broadcast_to(abi, bui.shape)
    _, _, hr, hi = lax.associative_scan(_cplx_combine, (ar, ai, bur, bui), axis=1)
    y = (jnp.einsum('nlgp,gcp->nlgc', hr, c_re.astype(F32))
         - jnp.einsum('nlgp,gcp->nlgc', hi, c_im.astype(F32)))
    y = y.reshape(n, l, S5_WIDTH) + d_skip.astype(F32) * u.astype(F32)
    y = jax.nn.gelu(y)
    y = y * jax.nn.sigmoid(y @ w_glu.astype(F32) + b_glu.astype(F32))
    return y, hr[:, -1], hi[:, -1]

def rglru_branch(xb, gb, conv_buf, h0, conv_w, conv_b, w_r, b_r, w_i, b_i, lam):
    n, l, _ = xb.shape
    xpad = jnp.concatenate([conv_buf.astype(xb.dtype), xb], axis=1)
    xc = conv_b + xpad[:, 0:l] * conv_w[0]
    for k in range(1, CONV_WIDTH):
        xc = xc + xpad[:, k:k + l] * conv_w[k]
    new_buf = xpad[:, l:]
    xh = xc.reshape(n, l, LRU_HEADS, LRU_HEAD_DIM)
    r = jax.nn.sigmoid((jnp.einsum('nlhi,hij->nlhj', xh, w_r).reshape(n, l, LRU_WIDTH) + b_r).astype(F32))
    ig = jax.nn.sigmoid((jnp.einsum('nlhi,hij->nlhj', xh, w_i).reshape(n, l, LRU_WIDTH) + b_i).astype(F32))
    log_a = -LRU_C * r * jax.nn.softplus(-lam.astype(F32))
    a = jnp.exp(log_a)
    mult = jnp.sqrt(-jnp.expm1(2.0 * log_a))
    bterm = mult * ig * xc.astype(F32)
    bterm = bterm.at[:, 0].add(a[:, 0] * h0.astype(F32))
    _, h = lax.associative_scan(_lin_combine, (a, bterm), axis=1)
    y = jax.nn.gelu(gb.astype(F32)) * h
    return y, h[:, -1], new_buf

def peer(xn, w_q, sub_keys, u_tab, v_tab):
    n, l, d = xn.shape
    t = xn.reshape(n * l, d)
    nt = n * l
    nb = -(-nt // PEER_BLOCK)
    t = jnp.pad(t, ((0, nb * PEER_BLOCK - nt), (0, 0))).reshape(nb, PEER_BLOCK, d)

    def block(tb):
        q = (tb @ w_q).reshape(PEER_BLOCK, PEER_HEADS, 2, KEY_HALF)
        s = jnp.einsum('thsk,hsnk->thsn', q, sub_keys).astype(F32)
        sv, si = lax.top_k(s, PEER_TOPK)
        cand = sv[:, :, 0, :, None] + sv[:, :, 1, None, :]
        cidx = si[:, :, 0, :, None] * N_KEYS + si[:, :, 1, None, :]
        cand = cand.reshape(PEER_BLOCK, PEER_HEADS, PEER_TOPK * PEER_TOPK)
        cidx = cidx.reshape(PEER_BLOCK, PEER_HEADS, PEER_TOPK * PEER_TOPK)
        top_s, pos = lax.top_k(cand, PEER_TOPK)
        idx = jnp.take_along_axis(cidx, pos, axis=-1)
        g = jax.nn.softmax(top_s, axis=-1)
        u = u_tab[idx]
        act = jax.nn.gelu(jnp.einsum('thkd,td->thk', u, tb).astype(F32))
        coef = (g * act).astype(tb.dtype)
        v = v_tab[idx]
        return jnp.einsum('thk,thkd->td', coef, v)

    out = lax.map(block, t)
    return out.reshape(nb * PEER_BLOCK, d)[:nt].reshape(n, l, d)

def _layer(x, p, h_s5_re, h_s5_im, h_lru, conv_buf,
           g_mix, w_in, s5_lam_re, s5_lam_im, s5_log_dt, s5_b_re, s5_b_im, s5_c_re, s5_c_im,
           s5_d, s5_w_glu, s5_b_glu, conv_w, conv_b, lru_w_r, lru_b_r, lru_w_i, lru_b_i, lru_lam,
           w_a_proj, w_b_proj, w_out, g_ffn, peer_w_q, peer_sub_keys, peer_u, peer_v,
           g_ple, w_ple, w_ple_gate):
    xn = rms_norm(x, g_mix)
    proj = xn @ w_in
    xa, xb, gb, ga_pre, gb_pre = jnp.split(proj, SPLITS, axis=-1)
    ya, s5r_new, s5i_new = s5_branch(xa, h_s5_re, h_s5_im, s5_lam_re, s5_lam_im, s5_log_dt,
                                     s5_b_re, s5_b_im, s5_c_re, s5_c_im, s5_d, s5_w_glu, s5_b_glu)
    yb, lru_new, conv_new = rglru_branch(xb, gb, conv_buf, h_lru, conv_w, conv_b,
                                         lru_w_r, lru_b_r, lru_w_i, lru_b_i, lru_lam)
    ya_d = ya.astype(x.dtype) @ w_a_proj
    yb_d = yb.astype(x.dtype) @ w_b_proj
    merged = jax.nn.sigmoid(ga_pre) * ya_d + jax.nn.sigmoid(gb_pre) * yb_d
    x = x + (merged @ w_out).astype(x.dtype)
    x = x + peer(rms_norm(x, g_ffn), peer_w_q, peer_sub_keys, peer_u, peer_v).astype(x.dtype)
    gate = jax.nn.sigmoid(rms_norm(x, g_ple) @ w_ple_gate)
    x = x + ((p.astype(x.dtype) @ w_ple) * gate).astype(x.dtype)
    return x, s5r_new, s5i_new, lru_new, conv_new

def setup_inputs(seed: int = 0) -> dict:
    key = jax.random.key(seed)
    ks = iter(jax.random.split(key, 64))

    def nrm(shape, scale):
        return jax.random.normal(next(ks), shape, F32) * scale

    def unif(shape, lo, hi):
        return jax.random.uniform(next(ks), shape, F32, lo, hi)

    n_idx = jnp.arange(S5_STATE, dtype=F32)
    lam_re = -0.5 + nrm((DEPTH, S5_GROUPS, S5_STATE), 0.01)
    lam_im = math.pi * n_idx + nrm((DEPTH, S5_GROUPS, S5_STATE), 0.01)
    a0 = unif((DEPTH, LRU_WIDTH), 0.9, 0.999)
    sig = a0 ** (1.0 / LRU_C)
    lru_lam = jnp.log(sig) - jnp.log1p(-sig)

    inp = {
        "x_prompt": nrm((BATCH, SEQ, D_MODEL), 1.0),
        "x_sample": nrm((DEC_BATCH, DEC_SEQ, D_MODEL), 1.0),
        "state_s5_re": nrm((DEPTH, DEC_BATCH, S5_GROUPS, S5_STATE), 0.1),
        "state_s5_im": nrm((DEPTH, DEC_BATCH, S5_GROUPS, S5_STATE), 0.1),
        "state_lru": nrm((DEPTH, DEC_BATCH, LRU_WIDTH), 0.5),
        "state_conv": nrm((DEPTH, DEC_BATCH, CONV_WIDTH - 1, LRU_WIDTH), 1.0),
        "p_prompt": nrm((DEPTH, BATCH, SEQ, PLE_DIM), 1.0),
        "p_sample": nrm((DEPTH, DEC_BATCH, DEC_SEQ, PLE_DIM), 1.0),
        "g_mix": 1.0 + nrm((DEPTH, D_MODEL), 0.02),
        "w_in": nrm((DEPTH, D_MODEL, IN_COLS), D_MODEL ** -0.5),
        "s5_lam_re": lam_re,
        "s5_lam_im": lam_im,
        "s5_log_dt": unif((DEPTH, S5_GROUPS), math.log(0.001), math.log(0.1)),
        "s5_b_re": nrm((DEPTH, S5_GROUPS, S5_STATE, S5_GROUP), (2 * S5_GROUP) ** -0.5),
        "s5_b_im": nrm((DEPTH, S5_GROUPS, S5_STATE, S5_GROUP), (2 * S5_GROUP) ** -0.5),
        "s5_c_re": nrm((DEPTH, S5_GROUPS, S5_GROUP, S5_STATE), (2 * S5_STATE) ** -0.5),
        "s5_c_im": nrm((DEPTH, S5_GROUPS, S5_GROUP, S5_STATE), (2 * S5_STATE) ** -0.5),
        "s5_d": nrm((DEPTH, S5_WIDTH), 1.0),
        "s5_w_glu": nrm((DEPTH, S5_WIDTH, S5_WIDTH), S5_WIDTH ** -0.5),
        "s5_b_glu": nrm((DEPTH, S5_WIDTH), 0.01),
        "conv_w": nrm((DEPTH, CONV_WIDTH, LRU_WIDTH), CONV_WIDTH ** -0.5),
        "conv_b": nrm((DEPTH, LRU_WIDTH), 0.01),
        "lru_w_r": nrm((DEPTH, LRU_HEADS, LRU_HEAD_DIM, LRU_HEAD_DIM), LRU_HEAD_DIM ** -0.5),
        "lru_b_r": nrm((DEPTH, LRU_WIDTH), 0.01),
        "lru_w_i": nrm((DEPTH, LRU_HEADS, LRU_HEAD_DIM, LRU_HEAD_DIM), LRU_HEAD_DIM ** -0.5),
        "lru_b_i": nrm((DEPTH, LRU_WIDTH), 0.01),
        "lru_lam": lru_lam,
        "w_a_proj": nrm((DEPTH, S5_WIDTH, D_MODEL), S5_WIDTH ** -0.5),
        "w_b_proj": nrm((DEPTH, LRU_WIDTH, D_MODEL), LRU_WIDTH ** -0.5),
        "w_out": nrm((DEPTH, D_MODEL, D_MODEL), D_MODEL ** -0.5),
        "g_ffn": 1.0 + nrm((DEPTH, D_MODEL), 0.02),
        "peer_w_q": nrm((DEPTH, D_MODEL, PEER_HEADS * QUERY_DIM), D_MODEL ** -0.5),
        "peer_sub_keys": nrm((DEPTH, PEER_HEADS, 2, N_KEYS, KEY_HALF), KEY_HALF ** -0.5),
        "peer_u": nrm((DEPTH, N_EXPERTS, D_MODEL), D_MODEL ** -0.5),
        "peer_v": nrm((DEPTH, N_EXPERTS, D_MODEL), 0.5),
        "g_ple": 1.0 + nrm((DEPTH, D_MODEL), 0.02),
        "w_ple": nrm((DEPTH, PLE_DIM, D_MODEL), PLE_DIM ** -0.5),
        "w_ple_gate": nrm((DEPTH, D_MODEL, D_MODEL), D_MODEL ** -0.5),
        "g_final": 1.0 + nrm((D_MODEL,), 0.02),
    }
    return inp

def reference(x_prompt, x_sample, state_s5_re, state_s5_im, state_lru, state_conv, p_prompt, p_sample,
              g_mix, w_in, s5_lam_re, s5_lam_im, s5_log_dt, s5_b_re, s5_b_im, s5_c_re, s5_c_im,
              s5_d, s5_w_glu, s5_b_glu, conv_w, conv_b, lru_w_r, lru_b_r, lru_w_i, lru_b_i, lru_lam,
              w_a_proj, w_b_proj, w_out, g_ffn, peer_w_q, peer_sub_keys, peer_u, peer_v,
              g_ple, w_ple, w_ple_gate, g_final):
    n_p = x_prompt.shape[0]
    z_s5 = jnp.zeros((n_p, S5_GROUPS, S5_STATE), F32)
    z_lru = jnp.zeros((n_p, LRU_WIDTH), F32)
    z_conv = jnp.zeros((n_p, CONV_WIDTH - 1, LRU_WIDTH), x_prompt.dtype)
    hp, hs = x_prompt, x_sample
    sp_re, sp_im, sp_lru, sp_conv = [], [], [], []
    ss_re, ss_im, ss_lru, ss_conv = [], [], [], []
    for i in range(DEPTH):
        lw = dict(g_mix=g_mix[i], w_in=w_in[i], s5_lam_re=s5_lam_re[i], s5_lam_im=s5_lam_im[i],
                  s5_log_dt=s5_log_dt[i], s5_b_re=s5_b_re[i], s5_b_im=s5_b_im[i], s5_c_re=s5_c_re[i],
                  s5_c_im=s5_c_im[i], s5_d=s5_d[i], s5_w_glu=s5_w_glu[i], s5_b_glu=s5_b_glu[i],
                  conv_w=conv_w[i], conv_b=conv_b[i], lru_w_r=lru_w_r[i], lru_b_r=lru_b_r[i],
                  lru_w_i=lru_w_i[i], lru_b_i=lru_b_i[i], lru_lam=lru_lam[i], w_a_proj=w_a_proj[i],
                  w_b_proj=w_b_proj[i], w_out=w_out[i], g_ffn=g_ffn[i], peer_w_q=peer_w_q[i],
                  peer_sub_keys=peer_sub_keys[i], peer_u=peer_u[i], peer_v=peer_v[i],
                  g_ple=g_ple[i], w_ple=w_ple[i], w_ple_gate=w_ple_gate[i])
        hp, a_re, a_im, a_lru, a_conv = _layer(hp, p_prompt[i], z_s5, z_s5, z_lru, z_conv, **lw)
        hs, b_re, b_im, b_lru, b_conv = _layer(hs, p_sample[i], state_s5_re[i], state_s5_im[i],
                                               state_lru[i], state_conv[i], **lw)
        sp_re.append(a_re); sp_im.append(a_im); sp_lru.append(a_lru); sp_conv.append(a_conv)
        ss_re.append(b_re); ss_im.append(b_im); ss_lru.append(b_lru); ss_conv.append(b_conv)
    y_prompt = rms_norm(hp, g_final)
    y_sample = rms_norm(hs, g_final)
    new_s5_re_prompt = jnp.stack(sp_re)
    new_s5_im_prompt = jnp.stack(sp_im)
    new_lru_prompt = jnp.stack(sp_lru)
    new_conv_prompt = jnp.stack(sp_conv)
    new_s5_re_sample = jnp.stack(ss_re)
    new_s5_im_sample = jnp.stack(ss_im)
    new_lru_sample = jnp.stack(ss_lru)
    new_conv_sample = jnp.stack(ss_conv)
    return (y_prompt, y_sample, new_s5_re_prompt, new_s5_im_prompt, new_lru_prompt, new_conv_prompt,
            new_s5_re_sample, new_s5_im_sample, new_lru_sample, new_conv_sample)


_drawn_inputs = setup_inputs


def setup_inputs(seed=0):
    import zlib

    import numpy as np

    out = dict(_drawn_inputs(seed))
    spreads = {}
    factors = {'s5_lam_re': 13.518,
     's5_b_glu': 19.863,
     'lru_b_r': 8.0,
     'lru_b_i': 8.0,
     'g_ple': 40.952,
     'g_final': 8.273}
    for name, (base, spread) in spreads.items():
        noise = np.random.default_rng([zlib.crc32(name.encode()), seed]).standard_normal(out[name].shape)
        drawn = base * np.exp(spread * noise) if base else spread * noise
        out[name] = __import__('jax').numpy.asarray(drawn.astype(out[name].dtype))
    for name, factor in factors.items():
        out[name] = (out[name] * factor).astype(out[name].dtype)
    return out
```

```python
import math
from contextlib import ExitStack

import concourse.bass as bass
from concourse import mybir

F32 = mybir.dt.float32
I32 = mybir.dt.int32
U32 = mybir.dt.uint32
ALU = mybir.AluOpType
ACT = mybir.ActivationFunctionType
AX = mybir.AxisListType

P = 128
D = 1024
KD = D // P
TP, TS = 1024, 64
T = TP + TS
SB, SL = 8, 8
NT = 9
CHUNKS = [(0, 384), (384, 384), (768, 320)]
S5W, NG, GC, NS = 512, 32, 16, 64
PAIRS = NG // 2
STEP = 8
NB = TP // STEP
SLOTS = NB + 1 + 2 * SB
HEADS, TOPK, NKEY = 8, 16, 128
RING = 8
EPS = 1e-6
MAGIC = 12582912.0
BELOW = -3.0e38
UNITS = NT * HEADS


def group_of(batch, q):
    return 8 * (batch // 2) + 2 * q + batch % 2


def groups(batch):
    return slice(group_of(batch, 0), group_of(batch, 3) + 1, 2)


def rows_of(t):
    return P if t < NT - 1 else TS


class Chain:

    def __init__(self, eng, sem):
        self.eng, self.sem, self.done, self.shift, self.outer = eng, sem, 0, 0, []

    def __call__(self, ins):
        ins.then_inc(self.sem, 1)
        self.done += 1
        self.eng.wait_ge(self.sem, self.shift + self.done)

    def enter(self, shift):
        self.outer.append((self.shift, self.done))
        self.shift = self.shift + shift

    def leave(self, trips, per):
        self.shift, start = self.outer.pop()
        assert self.done - start == per, (self.done - start, per)
        self.done = start + trips * per


def build(nc, a):
    ctx = ExitStack()
    base = (nc.sbuf_base + 31) // 32 * 32
    SMALL, XNT = base, base + 14336
    YAT = XNT + 34816
    R1 = YAT + 17408
    VREG = R1 + 34816
    CXR = VREG + 18560
    UC = CXR + 18432
    US = UC + 16384
    R2 = US + 16384
    END = nc.sbuf_usable_end

    def region(start, end):
        at = [start]

        def put(name, shape, dt=F32):
            n = 4
            for s in shape[1:]:
                n *= s
            t = nc.alloc_sbuf_tensor_at(name, shape, dt, offset=at[0])
            at[0] += (n + 31) // 32 * 32
            assert at[0] <= end, (name, at[0] - end)
            return t
        return put

    put = region(SMALL, XNT)
    ident = put("ident", [P, P])
    par = put("par", [P, 340])
    nconv = put("nconv", [P, KD, 1 + SB, 3])
    nlru = put("nlru", [P, KD, 1 + SB])
    sumsq = put("sumsq", [P, NT])
    rstd = put("rstd", [P, NT])
    sumsq2 = put("sumsq2", [P, NT])
    rstd2 = put("rstd2", [P, NT])
    spk = put("spk", [P, KD])
    hpar = put("hpar", [P, 8])
    A8 = put("A8", [P, 2, 2, PAIRS])
    cp_t = put("cp_t", [P, 2, 2, PAIRS])
    cp_u = put("cp_u", [P, 2, PAIRS])
    cs_t = put("cs_t", [P, SB, 2, PAIRS])
    dbc = put("dbc", [P, S5W])
    exs = put("exs", [P, 5, PAIRS])
    exi = put("exi", [P, PAIRS], I32)
    iota = put("iota", [P, TOPK])
    idxu = put("idxu", [P, 2, TOPK], U32)
    gw = put("gw", [P, 2, TOPK])
    dot = put("dot", [P, TOPK])
    act = put("act", [P, TOPK])
    gate_sum = put("gate_sum", [P, 4])
    top = put("top", [P, TOPK])
    pos = put("pos", [P, TOPK], U32)
    pab = put("pab", [P, 2, TOPK], U32)
    pabf = put("pabf", [P, 2, TOPK])
    pick = put("pick", [P, 2, TOPK])
    expt = put("expt", [P, TOPK])
    tail_s = put("tail_s", [P, 4])
    gmix, gple = par[:, 0:8], par[:, 8:16]
    bglu, lam = par[:, 16:20], par[:, 20:28]
    lrup = par[:, 28:84].rearrange("p (h n) -> p h n", h=KD)
    h0 = par[:, 84:148].rearrange("p (h b) -> p h b", h=KD)
    cst = par[:, 148:340].rearrange("p (h b n) -> p h b n", h=KD, b=SB)

    xnT = region(XNT, YAT)("xnT", [P, KD, T])
    xtok = region(YAT, VREG)("xtok", [P, NT, D])
    yaT = region(YAT, R1)("yaT", [P, 4, T])
    put = region(YAT, R1)
    Ksb = put("Ksb", [GC, NG, P])
    ybT = region(R1, VREG)("ybT", [P, KD, T])
    put = region(R1, VREG)
    M1 = put("M1", [P, NG, P])
    uT = put("uT", [P, NG, NB + SB])
    V = region(VREG, CXR)("V", [P, SLOTS, 2, PAIRS])
    M1T = region(VREG, CXR)("M1T", [P, PAIRS, 2, STEP, GC])
    sig = region(UC, R2)("sig", [P, 4, T])
    CX = region(CXR, UC)("CX", [P, PAIRS, 2, STEP + 1, GC])
    u_c = region(UC, US)("u_c", [P, NG, STEP, GC])
    u_s = region(US, R2)("u_s", [SB, NG, STEP, GC])
    put = region(US, R2)
    tmpb = put("tmpb", [P, PAIRS * (STEP + 1) * GC])
    s5w = put("s5w", [P, 4, PAIRS, GC])
    bb = put("bb", [P, 2, PAIRS, GC])
    put = region(R2, END)
    M3 = put("M3", [P, NG, P])
    wxa = put("wxa", [P, KD, S5W])
    ust = put("ust", [TS, S5W])
    s5s = put("s5s", [P, 24, PAIRS])
    pw = put("pw", [P, 2, PAIRS, STEP + 1])
    pwr = put("pwr", [P, 2, PAIRS, STEP])
    put = region(R2, END)
    w_xb = put("w_xb", [P, KD, P])
    w_gb = put("w_gb", [P, KD, P])
    w_ri = put("w_ri", [P, 2, P])
    xpad = put("xpad", [P, 3 + TP])
    xpads = put("xpads", [P, SB, 3 + SL])
    xc, rt, ig, av, dn, gg = (put(n, [P, T]) for n in ("xc", "rt", "ig", "av", "dn", "gg"))
    put = region(R2, END)
    wglu = put("wglu", [P, 4, S5W])
    y_c = put("y_c", [P, STEP, S5W])
    y_s = put("y_s", [SB, STEP, S5W])
    put = region(R2, END)
    w_ga = put("w_ga", [P, KD, P])
    w_ya = put("w_ya", [P, 4, P])
    w_gp = put("w_gp", [P, KD, P])
    w_yb = put("w_yb", [P, KD, P])
    sga, sgb, mg = (put(n, [P, T]) for n in ("sga", "sgb", "mg"))
    mgT = region(VREG, UC)("mgT", [P, KD, T])
    wout = region(UC, R2)("wout", [P, KD, D])
    x2 = region(XNT, R1)("x2", [P, NT, D])
    xn2T = region(R1, VREG)("xn2T", [P, KD, T])
    put = region(R2, END)
    gffn = put("gffn", [P, D])
    sv = put("sv", [P, UNITS + 1, 2, TOPK])
    si = put("si", [P, UNITS + 1, 2, TOPK])
    xr = put("xr", [P, 2, D])
    xn2s = put("xn2s", [P, 2, D])
    put = region(VREG, UC)
    keys = put("keys", [P, 2 * HEADS, NKEY])
    w_q = put("w_q", [P, 2, KD, P])
    qT = put("qT", [P, 2, T])
    put = region(UC, R2)
    svh = put("svh", [P, NT, 2, TOPK])
    sih = put("sih", [P, NT, 2, TOPK], U32)
    srep = put("srep", [P, 2, NKEY])
    put = region(XNT + 36864, R2)
    ring = put("ring", [P, RING, 2 * D])
    wgate = put("wgate", [P, KD, D])
    wple = put("wple", [P, 2, D])
    pT = put("pT", [P, 2, P])
    xn2c = put("xn2c", [P, D])
    dg = put("dg", [P, 4, P])
    cand = put("cand", [P, TOPK, TOPK])
    crep = put("crep", [P, TOPK, TOPK])
    hot = put("hot", [P, 2, TOPK, TOPK])
    put = region(R2 + 4096 + 18688 + 64, END)
    x3 = put("x3", [P, D])
    xn3 = put("xn3", [P, D])
    xn3T = put("xn3T", [P, KD, P])
    gfin = put("gfin", [P, D])

    psA = ctx.enter_context(nc.psum_tensor("psA", [P, 3, 512], F32))
    psB = ctx.enter_context(nc.psum_tensor("psB", [P, 3, 512], F32))
    psC = ctx.enter_context(nc.psum_tensor("psC", [P, 2, 512], F32))
    acc = psC[:, :, :].rearrange("p a n -> p (a n)")

    def alone(eng):
        eng.sem_inc(g.passed, 1)

    S = {}

    def sem(name):
        if name not in S:
            S[name] = ctx.enter_context(nc.semaphore(name))
        return S[name]

    def pieces(ps, buf, cols=CHUNKS):
        return [(ps[:, c, 0:n], buf[:, o:o + n]) for c, (o, n) in enumerate(cols)]

    names = """x_in par_in s5_in dbc_in wxa_in ident_ok xtok_ok ss_ok ms_ok sq_ok xn_ok xnT_tr xnT_ok
      s5_act s5_arg s5_ready m1_tr m1_ok k_mm k_ok m3_zero m3_in xa_mm xa_ok ust_ok scr_out us_in
      ut_tr ut_ok v_mm v_ok h0_in chain_ok y1_mm du_ok y1_ok st_out
      w_xb_in w_gb_in w_ri_in xb_mm xb_ok gb_mm gb_ok conv_ok gate_mm gate_ok tanh_ok den_ok sqrt_ok yb_ok hcol_ok
      y2_mm y2_ok gelu_ok ya_tr ya_ok glu_mm sig_ok ya_done wglu_in
      w_ga_in w_ya_in w_gp_in w_yb_in ga_mm ya_mm gp_mm yb_mm sga_ok mga_ok sgb_ok mg_ok
      wout_in xr_in gffn_in o_mm x2_ok ss2_ok ms2_ok sq2_ok xn2_ok xn2_tr xn2T_ok
      keys_in w_q0_in w_q1_in q_mm qT_ok sc_mm top_ok q_done
      wg_in wp_in gf_in pT_in idx_ok l2_top l2_exp dot_ok act_ok diag_ok slot_free acc_done x3_ok ss3_ok ms3_ok sq3_ok
      xn3_ok xn3_tr xn3T_ok gate3_mm gate3_ok ple_mm x4_ok ss4_ok ms4_ok sq4_ok y_ok y_out out_st
      passed v_tail v_own a_own p_own v_g g_sv""".split()
    for n in names:
        sem(n)
    gathered = [sem(f"gathered{i}") for i in range(RING)]
    g = type("Sems", (), {n: S[n] for n in names})

    block = ctx.enter_context(nc.Block())

    @block.sync
    def _(sp):
        sp.dma_start(xtok[:, 0:8, :], a["x"][0:TP, :].rearrange("(t p) d -> p t d", p=P)).then_inc(g.x_in, 16)
        sp.dma_start(xtok[0:TS, 8, :], a["x"][TP:T, :]).then_inc(g.x_in, 16)
        sp.dma_start(par[:], a["par"]).then_inc(g.par_in, 16)
        sp.dma_start(s5s[:, 0:3, :], a["s5_small"]).then_inc(g.s5_in, 16)
        sp.dma_start(s5w[:], a["s5_w"]).then_inc(g.s5_in, 16)
        sp.dma_start(dbc[:], a["s5_d"].partition_broadcast(P)).then_inc(g.dbc_in, 16)
        sp.dma_start(wxa[:], a["w_xa"]).then_inc(g.wxa_in, 16)
        sp.wait_ge(g.k_ok, 8)
        sp.wait_ge(g.m3_zero, 1)
        for j in range(STEP):
            sp.dma_start(M3[GC * j:GC * (j + 1), :, GC * j:], Ksb[:, :, 0:P - GC * j]).then_inc(g.m3_in, 16)
        sp.wait_ge(g.ust_ok, 1)
        sp.dma_start(a["scr"], ust[:]).then_inc(g.scr_out, 16)
        sp.wait_ge(g.scr_out, 16)
        sp.wait_ge(g.s5_ready, 2)
        sp.wait_ge(g.k_mm, 8)
        for grp in range(NG):
            sp.dma_start(u_s[:, grp], a["scr"].rearrange("(b j) (g c) -> b g j c", j=STEP, c=GC)[:, grp]).then_inc(g.us_in, 16)
        sp.wait_ge(g.m1_tr, 8)
        sp.dma_start(V[:, NB + 1:NB + 1 + SB, :, :], a["h_s5"]).then_inc(g.h0_in, 16)
        sp.wait_ge(g.y1_mm, 16)
        sp.wait_ge(g.ust_ok, 1)
        def load(w, src, n, got):
            sp.dma_start(w, a[src][bass.ds(n, 1)].rearrange("a p k c -> p (a k) c")).then_inc(got, 16)
        load(w_xb[:], "w_xb", 0, g.w_xb_in)
        load(w_gb[:], "w_gb", 0, g.w_gb_in)
        load(w_ri[:], "w_ri", 0, g.w_ri_in)
        with sp.Fori(1, KD) as h:
            sp.wait_ge(g.xb_mm, h)
            load(w_xb[:], "w_xb", h, g.w_xb_in)
            sp.wait_ge(g.gb_mm, h)
            load(w_gb[:], "w_gb", h, g.w_gb_in)
            sp.wait_ge(g.gate_mm, h * 6)
            load(w_ri[:], "w_ri", h, g.w_ri_in)
        sp.wait_ge(g.chain_ok, 2)
        sp.dma_start(a["o_s5"][:, 0:1], V[:, NB:NB + 1, :, :]).then_inc(g.st_out, 16)
        sp.dma_start(a["o_s5"][:, 1:1 + SB], V[:, NB + 1 + SB:SLOTS, :, :]).then_inc(g.st_out, 16)
        sp.wait_ge(g.yb_ok, KD)
        sp.dma_start(a["o_lru"], nlru[:]).then_inc(g.st_out, 16)
        sp.dma_start(a["o_conv"], nconv[:]).then_inc(g.st_out, 16)
        sp.dma_start(wglu[:], a["w_glu"]).then_inc(g.wglu_in, 16)
        sp.wait_ge(g.glu_mm, 4)
        sp.wait_ge(g.ya_done, 1)
        sp.dma_start(wout[:], a["w_out"]).then_inc(g.wout_in, 16)
        slots = ((w_ga, "w_ga", g.w_ga_in, g.ga_mm), (w_ya, "w_ya", g.w_ya_in, g.ya_mm),
                 (w_gp, "w_gp", g.w_gp_in, g.gp_mm), (w_yb, "w_yb", g.w_yb_in, g.yb_mm))
        for w, src, got, used in slots:
            load(w[:], src, 0, got)
        with sp.Fori(1, KD) as m:
            for w, src, got, used in slots:
                sp.wait_ge(used, m)
                load(w[:], src, m, got)
        sp.wait_ge(g.mg_ok, KD + 1)
        sp.dma_start(gffn[:], a["g_ffn"].partition_broadcast(P)).then_inc(g.gffn_in, 16)
        for t in range(NT):
            if t >= 2:
                sp.wait_ge(g.x2_ok, t - 1)
            sp.dma_start(xr[0:rows_of(t), t % 2, :], a["x"][P * t:P * t + rows_of(t), :]).then_inc(sem(f"xr_in{t % 2}"), 16)
        sp.wait_ge(g.o_mm, NT)
        sp.dma_start(keys[:], a["keys"]).then_inc(g.keys_in, 16)
        load(w_q[:, 0], "w_q", 0, g.w_q0_in)
        load(w_q[:, 1], "w_q", 1, g.w_q1_in)
        with sp.Fori(1, HEADS) as h:
            for s, got in ((0, g.w_q0_in), (1, g.w_q1_in)):
                sp.wait_ge(g.q_mm, h * 2 + s - 1)
                load(w_q[:, s], "w_q", h * 2 + s, got)
        sp.wait_ge(g.sc_mm, 2 * HEADS)
        sp.wait_ge(g.q_done, 1)
        sp.dma_start(wgate[:], a["w_gate"]).then_inc(g.wg_in, 16)
        sp.dma_start(wple[:], a["w_ple"]).then_inc(g.wp_in, 16)
        sp.dma_start(gfin[:], a["g_final"].partition_broadcast(P)).then_inc(g.y_out, 16)
        sp.dma_start(pT[:], a["p_T"][:, :, 0:P]).then_inc(g.pT_in, 16)

        def store(t, rows):
            sp.wait_ge(g.y_ok, t + 1)
            sp.dma_start(a["o_y"][bass.ds(t * P, rows), :], xn3[0:rows, :]).then_inc(g.y_out, 16)
        with sp.Fori(1, NT - 1) as t:
            sp.wait_ge(g.ple_mm, t)
            sp.dma_start(pT[:], a["p_T"][:, :, bass.ds(t * P, P)]).then_inc(g.pT_in, 16)
            store(t - 1, P)
        sp.wait_ge(g.ple_mm, NT - 1)
        sp.dma_start(pT[:, :, 0:TS], a["p_T"][:, :, TP:T]).then_inc(g.pT_in, 16)
        store(NT - 2, P)
        store(NT - 1, TS)
        sp.wait_ge(g.y_out, 16 * (NT + 1))
        sp.wait_ge(g.st_out, 64)

    @block.gpsimd
    def _(pool):
        own = Chain(pool, g.p_own)
        own(nc.gpsimd.memset(ident[:], 0.0))
        nc.gpsimd.affine_select(out=ident[:], in_=ident[:], compare_op=ALU.not_equal, fill=1.0, base=0,
                                pattern=[[-1, P]], channel_multiplier=1).then_inc(g.ident_ok, 1)
        own(nc.gpsimd.iota(iota[:], pattern=[[1, TOPK]], base=0, channel_multiplier=0,
                           allow_small_or_imprecise_dtypes=True))
        nc.gpsimd.memset(M3[:], 0.0).then_inc(g.m3_zero, 1)
        pool.wait_ge(g.v_ok, PAIRS + 1)
        pool.wait_ge(g.h0_in, 16)

        with pool.Fori(0, NB) as c:
            own.enter(c * 3)
            prev = V[:, bass.ds(c, 1)].rearrange("p a i g -> p (a i) g")
            here = V[:, bass.ds(c + 1, 1)].rearrange("p a i g -> p (a i) g")
            own(nc.gpsimd.tensor_tensor(cp_t[:], A8[:], prev.unsqueeze(1).broadcast_to([P, 2, 2, PAIRS]), ALU.mult))
            own(nc.gpsimd.tensor_tensor(cp_u[:], cp_t[:, :, 0, :], cp_t[:, :, 1, :], ALU.add))
            own(nc.gpsimd.tensor_tensor(here, here, cp_u[:], ALU.add))
        own.leave(NB, 3)
        nc.gpsimd.tensor_copy(cp_u[:], cp_u[:]).then_inc(g.chain_ok, 1)
        ini = V[:, NB + 1:NB + 1 + SB]
        fin = V[:, NB + 1 + SB:SLOTS]
        for o in range(2):
            own(nc.gpsimd.tensor_tensor(cs_t[:], ini, A8[:, o:o + 1].broadcast_to([P, SB, 2, PAIRS]), ALU.mult))
            for i in range(2):
                own(nc.gpsimd.tensor_tensor(fin[:, :, o], fin[:, :, o], cs_t[:, :, i], ALU.add))
        nc.gpsimd.tensor_copy(cp_u[:], cp_u[:]).then_inc(g.chain_ok, 1)
        pool.wait_ge(g.x2_ok, NT)
        nc.gpsimd.memset(sv[:, UNITS - HEADS:UNITS + 1], 0.0).then_inc(g.g_sv, 1)
        nc.gpsimd.memset(si[:, UNITS - HEADS:UNITS + 1], 0.0).then_inc(g.g_sv, 1)

        def gather(u, s, rows):
            pool.wait_ge(g.idx_ok, u + 1)
            for k in range(TOPK):
                pool.wait_ge(g.slot_free, u * TOPK + (k + 1))
                alone(pool)
                pool.indirect_dma_start(
                    out=ring[0:rows, k % RING, :], out_offset=None, in_=a["uv"],
                    in_offset=bass.IndirectOffsetOnAxis(ap=idxu[0:rows, s, k:k + 1], axis=0),
                ).then_inc(gathered[k % RING], 16)
        with pool.Fori(0, (UNITS - HEADS) // 2) as w:
            for s in range(2):
                gather(w * 2 + s, s, P)
        with pool.Fori((UNITS - HEADS) // 2, UNITS // 2) as w:
            for s in range(2):
                gather(w * 2 + s, s, TS)

    @block.tensor
    def _(pe):
        def transposes(dst, srcs, done=None):
            for d, s in zip(dst, srcs):
                k = s.shape[0]
                b = s.start_partition if not callable(s.start_partition) else s.start_partition()
                ins = nc.tensor.transpose(d, s, ident[b:b + k, b:b + k])
            if done is not None:
                ins.then_inc(done, 1)

        def product(ps, w, cols, moving, done):
            n = w.shape[1]
            for c, (o, width) in enumerate(CHUNKS):
                for k in range(n):
                    ins = nc.tensor.matmul(ps[:, c, 0:width], w[:, k, cols], moving[:, k, o:o + width],
                                           start=(k == 0), stop=(k == n - 1))
            ins.then_inc(done, 1)

        pe.wait_ge(g.ident_ok, 1)
        for t in range(NT):
            n = rows_of(t)
            pe.wait_ge(g.xn_ok, t + 1)
            if t >= 2:
                pe.wait_ge(g.xnT_ok, t - 1)
            ps = (psA, psB)[t % 2]
            transposes([ps[:, k // 4, P * (k % 4):P * (k % 4) + n] for k in range(KD)],
                       [xtok[0:n, t, P * k:P * (k + 1)] for k in range(KD)], g.xnT_tr)
        pe.wait_ge(g.xnT_ok, NT)
        pe.wait_ge(g.wxa_in, 16)
        for j in range(STEP):
            if j >= 2:
                pe.wait_ge(g.xa_ok, j - 1)
            for k in range(KD):
                ins = nc.tensor.matmul(psC[:, j % 2, :], xnT[:, k, j:TP:STEP], wxa[:, k, :],
                                       start=(k == 0), stop=(k == KD - 1))
            ins.then_inc(g.xa_mm, 1)
        pe.wait_ge(g.xa_ok, STEP - 1)
        for k in range(KD):
            ins = nc.tensor.matmul(psC[0:TS, 0, :], xnT[:, k, TP:T], wxa[:, k, :], start=(k == 0), stop=(k == KD - 1))
        ins.then_inc(g.xa_mm, 1)
        pe.wait_ge(g.s5_ready, 1)
        for b in range(8):
            if b >= 2:
                pe.wait_ge(g.m1_ok, b - 1)
            for q in range(4):
                grp = group_of(b, q)
                lo = NS * (grp % 2)
                for ri in range(2):
                    ins = nc.tensor.transpose(
                        psA[:, b % 2, P * q + NS * ri:P * q + NS * (ri + 1)],
                        M1T[lo:lo + NS, grp // 2, ri].rearrange("p j c -> p (j c)"), ident[lo:lo + NS, lo:lo + NS])
            ins.then_inc(g.m1_tr, 1)
        pe.wait_ge(g.s5_ready, 2)
        for b in range(8):
            if b >= 2:
                pe.wait_ge(g.k_ok, b - 1)
            for q in range(4):
                grp = group_of(b, q)
                lo = NS * (grp % 2)
                for ri in range(2):
                    ins = nc.tensor.matmul(
                        psB[0:GC, b % 2, P * q:P * (q + 1)], bb[lo:lo + NS, ri, grp // 2, :],
                        CX[lo:lo + NS, grp // 2, ri, 0:STEP, :].rearrange("p n c -> p (n c)"),
                        start=(ri == 0), stop=(ri == 1))
            ins.then_inc(g.k_mm, 1)
        pe.wait_ge(g.xa_ok, STEP + 1)
        pe.wait_ge(g.m1_ok, 8)
        for b in range(8):
            if b >= 2:
                pe.wait_ge(g.ut_ok, b - 1)
            for q in range(4):
                grp = group_of(b, q)
                ins = nc.tensor.transpose(psA[:, b % 2, P * q:P * (q + 1)], u_c[:, grp].rearrange("p j c -> p (j c)"), ident[:])
            ins.then_inc(g.ut_tr, 1)
        pe.wait_ge(g.us_in, 16 * NG)
        for grp in range(NG):
            ins = nc.tensor.transpose(psA[:, 2, SB * grp:SB * (grp + 1)], u_s[:, grp].rearrange("p j c -> p (j c)"),
                                      ident[0:SB, 0:SB])
        ins.then_inc(g.ut_tr, 1)
        pe.wait_ge(g.ut_ok, 9)
        for q in range(PAIRS):
            if q >= 2:
                pe.wait_ge(g.v_ok, q - 1)
            for h in range(2):
                for ri in range(2):
                    ins = nc.tensor.matmul(psC[NS * h:NS * (h + 1), q % 2, 256 * ri:256 * ri + NB + SB],
                                           M1[:, 2 * q + h, NS * ri:NS * (ri + 1)], uT[:, 2 * q + h, :],
                                           start=True, stop=True, skip_group_check=True)
            ins.then_inc(g.v_mm, 1)
        pe.wait_ge(g.m3_in, 16 * STEP)
        for b in range(8):
            if b >= 2:
                pe.wait_ge(g.y1_ok, 2 * b - 2)
            for q in range(4):
                grp = group_of(b, q)
                ins = nc.tensor.matmul(psA[:, b % 2, P * q:P * (q + 1)], uT[:, grp, 0:NB], M3[:, grp, :],
                                       start=True, stop=True)
            ins.then_inc(g.y1_mm, 1)
            for q in range(4):
                grp = group_of(b, q)
                ins = nc.tensor.matmul(psB[0:SB, b % 2, P * q:P * (q + 1)], uT[:, grp, NB:NB + SB], M3[:, grp, :],
                                       start=True, stop=True)
            ins.then_inc(g.y1_mm, 1)
        pe.wait_ge(g.y1_ok, 16)
        with pe.Fori(0, KD) as h:
            pe.wait_ge(g.w_xb_in, h * 16 + 16)
            product(psA, w_xb, slice(0, P), xnT, g.xb_mm)
            pe.wait_ge(g.w_gb_in, h * 16 + 16)
            product(psB, w_gb, slice(0, P), xnT, g.gb_mm)
            pe.wait_ge(g.conv_ok, h + 1)
            pe.wait_ge(g.w_ri_in, h * 16 + 16)
            for c, (o, n) in enumerate(CHUNKS):
                for r in range(2):
                    if c > 0:
                        pe.wait_ge(g.gate_ok, h * 6 + (2 * c + r - 1))
                    nc.tensor.matmul(psC[:, r, 0:n], w_ri[:, r, :], xc[:, o:o + n], start=True,
                                     stop=True).then_inc(g.gate_mm, 1)
            pe.wait_ge(g.xb_ok, h + 1)
            pe.wait_ge(g.gb_ok, h + 1)
        pe.wait_ge(g.chain_ok, 2)
        pe.wait_ge(g.xb_ok, KD)
        pe.wait_ge(g.gb_ok, KD)
        for b in range(8):
            if b >= 2:
                pe.wait_ge(g.y2_ok, 2 * b - 2)
            for ps, n, s0 in ((psA, NB, 0), (psB, SB, NB + 1)):
                for q in range(4):
                    grp = group_of(b, q)
                    lo = NS * (grp % 2)
                    for ri in range(2):
                        ins = nc.tensor.matmul(
                            ps[0:n, b % 2, P * q:P * (q + 1)], V[lo:lo + NS, s0:s0 + n, ri, grp // 2],
                            CX[lo:lo + NS, grp // 2, ri, 1:STEP + 1, :].rearrange("p n c -> p (n c)"),
                            start=(ri == 0), stop=(ri == 1))
                ins.then_inc(g.y2_mm, 1)
        pe.wait_ge(g.gelu_ok, 2)
        pe.wait_ge(g.gate_ok, 6 * KD)
        for j in range(STEP):
            if j >= 2:
                pe.wait_ge(g.ya_ok, j - 1)
            transposes([psC[:, j % 2, P * f:P * (f + 1)] for f in range(4)],
                       [y_c[:, j, P * f:P * (f + 1)] for f in range(4)], g.ya_tr)
        for j in range(STEP):
            for f in range(4):
                o = (f * STEP + j) * SB
                ins = nc.tensor.transpose(psA[:, 2, o:o + SB], y_s[:, j, P * f:P * (f + 1)], ident[0:SB, 0:SB])
        ins.then_inc(g.ya_tr, 1)
        pe.wait_ge(g.ya_ok, STEP + 1)
        pe.wait_ge(g.wglu_in, 16)
        for m in range(4):
            ps = (psA, psB)[m % 2]
            if m >= 2:
                pe.wait_ge(g.sig_ok, m - 1)
            product(ps, wglu, slice(P * m, P * (m + 1)), yaT, g.glu_mm)
        pe.wait_ge(g.ya_done, 1)
        pe.wait_ge(g.yb_ok, KD)
        with pe.Fori(0, KD) as m:
            pe.wait_ge(g.w_ga_in, m * 16 + 16)
            product(psA, w_ga, slice(0, P), xnT, g.ga_mm)
            pe.wait_ge(g.mg_ok, m + 1)
            pe.wait_ge(g.w_ya_in, m * 16 + 16)
            product(psB, w_ya, slice(0, P), yaT, g.ya_mm)
            pe.wait_ge(g.sga_ok, m + 1)
            pe.wait_ge(g.w_gp_in, m * 16 + 16)
            product(psA, w_gp, slice(0, P), xnT, g.gp_mm)
            pe.wait_ge(g.mga_ok, m + 1)
            pe.wait_ge(g.w_yb_in, m * 16 + 16)
            product(psB, w_yb, slice(0, P), ybT, g.yb_mm)
            pe.wait_ge(g.sgb_ok, m + 1)
        pe.wait_ge(g.mg_ok, KD + 1)
        pe.wait_ge(g.wout_in, 16)

        def x2_transposes(t):
            n = rows_of(t)
            pe.wait_ge(g.xn2_ok, t + 1)
            if t >= 1:
                pe.wait_ge(g.xn2T_ok, t)
            transposes([psA[:, k // 4, P * (k % 4):P * (k % 4) + n] for k in range(KD)],
                       [xn2s[0:n, t % 2, P * k:P * (k + 1)] for k in range(KD)], g.xn2_tr)
        for t in range(NT):
            n = rows_of(t)
            ps = (psC, psB)[t % 2]
            if t >= 2:
                pe.wait_ge(g.x2_ok, t - 1)
            for half in range(2):
                for k in range(KD):
                    ins = nc.tensor.matmul(ps[0:n, half, :], mgT[:, k, P * t:P * t + n],
                                           wout[:, k, 512 * half:512 * (half + 1)], start=(k == 0), stop=(k == KD - 1))
            ins.then_inc(g.o_mm, 1)
            if t >= 1:
                x2_transposes(t - 1)
        x2_transposes(NT - 1)
        pe.wait_ge(g.xn2T_ok, NT)
        pe.wait_ge(g.keys_in, 16)
        with pe.Fori(0, HEADS) as h:
            for s, got in ((0, g.w_q0_in), (1, g.w_q1_in)):
                pe.wait_ge(got, h * 16 + 16)
                product(psA, w_q[:, s], slice(0, P), xn2T, g.q_mm)
                pe.wait_ge(g.qT_ok, h * 2 + (s + 1))
                pe.wait_ge(g.top_ok, h * 2 + s + 1)
                for t in range(NT):
                    n = rows_of(t)
                    ins = nc.tensor.matmul(psB[0:n, t // 4, P * (t % 4):P * (t % 4 + 1)], qT[:, s, P * t:P * t + n],
                                           keys[:, bass.ds(h * 2 + s, 1), :].rearrange("p a n -> p (a n)"),
                                           start=True, stop=True)
                ins.then_inc(g.sc_mm, 1)
        pe.wait_ge(g.q_done, 1)
        nc.tensor.transpose(psA[:, 0, 0:P], ident[:], ident[:]).then_inc(g.slot_free, RING)

        def experts(u, rows, last=False, between={}):
            for k in range(TOPK):
                pe.wait_ge(g.diag_ok, u * TOPK + (k + 1))
                alone(pe)
                for half in range(2):
                    ins = nc.tensor.matmul(acc[0:rows, 512 * half:512 * (half + 1)], dg[0:rows, k % 4, 0:rows],
                                           ring[0:rows, k % RING, D + 512 * half:D + 512 * (half + 1)],
                                           start=False, stop=(last and k == TOPK - 1))
                ins.then_inc(g.slot_free, 1)
                for step in between.get(k, ()):
                    step()

        def embedding(t, rows):
            def turn():
                pe.wait_ge(g.xn3_ok, t + 1)
                alone(pe)
                transposes([psA[:, k // 4, P * (k % 4):P * (k % 4) + rows] for k in range(KD)],
                           [xn3[0:rows, P * k:P * (k + 1)] for k in range(KD)], g.xn3_tr)

            def step(ps, x, w, n, half, k, first, done):
                def run():
                    if first:
                        pe.wait_ge(g.pT_in, t * 16 + 16)
                        pe.wait_ge(g.xn3T_ok, t + 1)
                        alone(pe)
                    ins = nc.tensor.matmul(ps[0:rows, half, :], x[:, k, 0:rows], w[:, k, 512 * half:512 * (half + 1)],
                                           start=(k == 0), stop=(k == n - 1))
                    if half == 1 and k == n - 1:
                        ins.then_inc(done, 1)
                return run
            todo = [step(psA, pT, wple, 2, half, k, half + k == 0, g.ple_mm) for half in range(2) for k in range(2)]
            todo += [step(psB, xn3T, wgate, KD, half, k, False, g.gate3_mm) for half in range(2) for k in range(KD)]
            return turn, todo

        def tile(t, rows, before):
            if before:
                pe.wait_ge(g.x3_ok, t)
                alone(pe)
            for half in range(2):
                nc.tensor.matmul(acc[0:rows, 512 * half:512 * (half + 1)], ident[0:rows, 0:rows],
                                 x2[0:rows, bass.ds(t, 1), 512 * half:512 * (half + 1)].rearrange("p a n -> p (a n)"),
                                 start=True, stop=False)
            first, second = {}, {}
            if before:
                turn, todo = embedding(t - 1, P)
                first[6] = [turn]
                for k in range(9, TOPK):
                    first[k] = [todo.pop(0), todo.pop(0)]
                for k in range(3):
                    second[k] = [todo.pop(0), todo.pop(0)]
                assert not todo
            experts(t * HEADS, rows, between=first)
            experts(t * HEADS + 1, rows, between=second)
            with pe.Fori(1, HEADS // 2 - 1) as w:
                for s in range(2):
                    experts(t * HEADS + w * 2 + s, rows)
            experts(t * HEADS + 6, rows)
            experts(t * HEADS + 7, rows, last=True)
            nc.tensor.transpose(psB[0:rows, 2, 0:rows], ident[0:rows, 0:rows], ident[0:rows, 0:rows]).then_inc(g.acc_done, 1)

        pe.wait_ge(g.wg_in, 16)
        pe.wait_ge(g.wp_in, 16)
        tile(0, P, False)
        with pe.Fori(1, NT - 1) as t:
            tile(t, P, True)
        tile(NT - 1, TS, True)
        turn, todo = embedding(NT - 1, TS)
        for step in [turn] + todo:
            step()

    @block.scalar
    def _(sc):
        own = Chain(sc, g.a_own)
        sc.wait_ge(g.x_in, 32)
        for t in range(NT):
            n = rows_of(t)
            own(nc.scalar.activation(acc[0:n, :], xtok[0:n, t, :], ACT.Square, accum_out=sumsq[0:n, t:t + 1]))
        nc.scalar.activation(sumsq[:, 0:1], sumsq[:, 0:1], ACT.Copy).then_inc(g.ss_ok, 1)
        sc.wait_ge(g.ms_ok, 1)
        nc.scalar.activation(rstd[:], rstd[:], ACT.Sqrt).then_inc(g.sq_ok, 1)
        sc.wait_ge(g.s5_arg, 1)
        nc.scalar.activation(s5s[:, 8:10, :], s5s[:, 6:8, :], ACT.Sin).then_inc(g.s5_act, 1)
        for j in range(STEP):
            sc.wait_ge(g.xa_mm, j + 1)
            nc.scalar.activation(u_c[:, :, j, :], psC[:, j % 2, :].rearrange("p (g c) -> p g c", g=NG), ACT.Copy).then_inc(g.xa_ok, 1)
        sc.wait_ge(g.xa_mm, STEP + 1)
        nc.scalar.activation(ust[:], psC[0:TS, 0, :], ACT.Copy).then_inc(g.ust_ok, 1)
        sc.wait_ge(g.ust_ok, 1)
        nc.scalar.activation(tail_s[0:1, 0:1], ust[0:1, 0:1], ACT.Copy).then_inc(g.xa_ok, 1)
        sc.wait_ge(g.xnT_ok, NT)
        for b in range(8):
            sc.wait_ge(g.m1_tr, b + 1)
            nc.scalar.activation(M1[:, groups(b), :], psA[:, b % 2, :].rearrange("p (q n) -> p q n", q=4),
                                 ACT.Copy).then_inc(g.m1_ok, 1)
        for b in range(8):
            sc.wait_ge(g.k_mm, b + 1)
            nc.scalar.activation(Ksb[:, groups(b), :], psB[0:GC, b % 2, :].rearrange("p (q n) -> p q n", q=4),
                                 ACT.Copy).then_inc(g.k_ok, 1)
        for b in range(8):
            sc.wait_ge(g.ut_tr, b + 1)
            nc.scalar.activation(uT[:, groups(b), 0:NB], psA[:, b % 2, :].rearrange("p (q n) -> p q n", q=4),
                                 ACT.Copy).then_inc(g.ut_ok, 1)
        sc.wait_ge(g.ut_tr, 9)
        nc.scalar.activation(uT[:, :, NB:NB + SB], psA[:, 2, 0:NG * SB].rearrange("p (q n) -> p q n", q=NG),
                             ACT.Copy).then_inc(g.ut_ok, 1)
        with sc.Fori(0, KD) as h:
            sc.wait_ge(g.xb_mm, h + 1)
            nc.scalar.activation(xpad[:, 3:387], psA[:, 0, 0:384], ACT.Copy)
            nc.scalar.activation(xpad[:, 387:771], psA[:, 1, 0:384], ACT.Copy)
            nc.scalar.activation(xpad[:, 771:1027], psA[:, 2, 0:256], ACT.Copy)
            nc.scalar.activation(xpads[:, :, 3:11], psA[:, 2, 256:320].rearrange("p (b l) -> p b l", b=SB),
                                 ACT.Copy).then_inc(g.xb_ok, 1)
            sc.wait_ge(g.gb_mm, h + 1)
            for c, (src, dst) in enumerate(pieces(psB, gg)):
                ins = nc.scalar.activation(dst, src, ACT.Gelu_apprx_tanh)
            ins.then_inc(g.gb_ok, 1)
            sc.wait_ge(g.hcol_ok, h + 1)
            for c, (o, n) in enumerate(CHUNKS):
                for r, buf in ((0, rt), (1, ig)):
                    sc.wait_ge(g.gate_mm, h * 6 + (2 * c + r + 1))
                    nc.scalar.activation(buf[:, o:o + n], psC[:, r, 0:n], ACT.Sigmoid,
                                         bias=hpar[:, 5 + r:6 + r]).then_inc(g.gate_ok, 1)
            sc.wait_ge(g.gate_ok, h * 6 + 6)
            nc.scalar.activation(rt[:], rt[:], ACT.Tanh, scale=hpar[:, 7:8]).then_inc(g.tanh_ok, 1)
            sc.wait_ge(g.den_ok, h + 1)
            nc.scalar.activation(rt[:], rt[:], ACT.Sqrt, scale=-4.0).then_inc(g.sqrt_ok, 1)
            sc.wait_ge(g.yb_ok, h + 1)
        sc.wait_ge(g.y2_ok, 16)
        nc.scalar.activation(y_c[:].rearrange("p j (g c) -> p g j c", g=NG), u_c[:], ACT.Gelu_apprx_tanh).then_inc(g.gelu_ok, 1)
        nc.scalar.activation(y_s[:].rearrange("p j (g c) -> p g j c", g=NG), u_s[:], ACT.Gelu_apprx_tanh).then_inc(g.gelu_ok, 1)
        for j in range(STEP):
            sc.wait_ge(g.ya_tr, j + 1)
            nc.scalar.activation(yaT[:, :, j:TP:STEP], psC[:, j % 2, :].rearrange("p (f n) -> p f n", f=4),
                                 ACT.Copy).then_inc(g.ya_ok, 1)
        sc.wait_ge(g.ya_tr, STEP + 1)
        for f in range(4):
            ins = nc.scalar.activation(
                yaT[:, f, TP:T].rearrange("p (b j) -> p j b", b=SB),
                psA[:, 2, f * TS:(f + 1) * TS].rearrange("p (j b) -> p j b", j=STEP), ACT.Copy)
        ins.then_inc(g.ya_ok, 1)
        for m in range(4):
            sc.wait_ge(g.glu_mm, m + 1)
            ps = (psA, psB)[m % 2]
            for src, dst in pieces(ps, sig[:, m, :]):
                ins = nc.scalar.activation(dst, src, ACT.Sigmoid, bias=bglu[:, m:m + 1])
            ins.then_inc(g.sig_ok, 1)
        with sc.Fori(0, KD) as m:
            sc.wait_ge(g.ga_mm, m + 1)
            sc.wait_ge(g.mg_ok, m + 1)
            for src, dst in pieces(psA, sga):
                ins = nc.scalar.activation(dst, src, ACT.Sigmoid)
            ins.then_inc(g.sga_ok, 1)
            sc.wait_ge(g.gp_mm, m + 1)
            for src, dst in pieces(psA, sgb):
                ins = nc.scalar.activation(dst, src, ACT.Sigmoid)
            ins.then_inc(g.sgb_ok, 1)
        for t in range(NT + 1):
            if t < NT:
                n = rows_of(t)
                sc.wait_ge(g.x2_ok, t + 1)
                if t >= 2:
                    sc.wait_ge(g.xn2_tr, t - 1)
                own(nc.scalar.activation(xn2s[0:n, t % 2, :], x2[0:n, t, :], ACT.Square,
                                         accum_out=sumsq2[0:n, t:t + 1]))
                nc.scalar.activation(sumsq2[0:n, t:t + 1], sumsq2[0:n, t:t + 1], ACT.Copy).then_inc(g.ss2_ok, 1)
                sc.wait_ge(g.ms2_ok, t + 1)
                nc.scalar.activation(rstd2[0:n, t:t + 1], rstd2[0:n, t:t + 1], ACT.Sqrt).then_inc(g.sq2_ok, 1)
            if t >= 1:
                n = rows_of(t - 1)
                sc.wait_ge(g.xn2_tr, t)
                for b in range(2):
                    ins = nc.scalar.activation(xn2T[:, 4 * b:4 * b + 4, P * (t - 1):P * (t - 1) + n],
                                               psA[:, b, :].rearrange("p (k n) -> p k n", k=4)[:, :, 0:n], ACT.Copy)
                ins.then_inc(g.xn2T_ok, 1)
        with sc.Fori(0, HEADS) as h:
            for s in range(2):
                sc.wait_ge(g.q_mm, h * 2 + (s + 1))
                for src, dst in pieces(psA, qT[:, s, :]):
                    ins = nc.scalar.activation(dst, src, ACT.Copy)
                ins.then_inc(g.qT_ok, 1)

        def softmax_exp(u):
            sc.wait_ge(g.l2_top, u + 1)
            nc.scalar.activation(expt[:], top[:], ACT.Exp, bias=gate_sum[:, 0:1],
                                 accum_out=gate_sum[:, 1:2])
            nc.scalar.activation(gate_sum[:, 3:4], gate_sum[:, 0:1], ACT.Copy).then_inc(g.l2_exp, 1)

        def activations(u, rows, between={}):
            for q in range(TOPK // 2):
                sc.wait_ge(g.dot_ok, u * 8 + (q + 1))
                nc.scalar.activation(act[0:rows, 2 * q:2 * q + 2], dot[0:rows, 2 * q:2 * q + 2],
                                     ACT.Gelu_apprx_tanh).then_inc(g.act_ok, 1)
                if q == 1:
                    softmax_exp(u + 1)
                for step in between.get(q, ()):
                    step()

        def embedding(t, rows):
            def out():
                sc.wait_ge(g.acc_done, t + 1)
                nc.scalar.activation(x3[0:rows, :], acc[0:rows, :], ACT.Copy).then_inc(g.x3_ok, 1)

            def squares(ready):
                def run():
                    if ready is None:
                        sc.wait_ge(g.x3_ok, t + 1)
                        sc.wait_ge(g.y_out, t * 16 + 16)
                    else:
                        sc.wait_ge(ready, t + 1)
                    nc.scalar.activation(xn3[0:rows, :], x3[0:rows, :], ACT.Square, accum_out=tail_s[0:rows, 0:1])
                    nc.scalar.activation(tail_s[0:rows, 3:4], x3[0:rows, 0:1], ACT.Copy).then_inc(
                        g.ss3_ok if ready is None else g.ss4_ok, 1)
                return run

            def root(ready, done):
                def run():
                    sc.wait_ge(ready, t + 1)
                    nc.scalar.activation(tail_s[0:rows, 1:2], tail_s[0:rows, 1:2], ACT.Sqrt).then_inc(done, 1)
                return run

            def gate():
                sc.wait_ge(g.gate3_mm, t + 1)
                nc.scalar.activation(xn3[0:rows, :], psB[0:rows, 0:2, :].rearrange("p a n -> p (a n)"),
                                     ACT.Sigmoid).then_inc(g.gate3_ok, 1)
            return (out, squares(None), root(g.ms3_ok, g.sq3_ok), gate, squares(g.x4_ok), root(g.ms4_ok, g.sq4_ok))

        def tile(t, rows, before):
            first, second = {}, {}
            if before:
                out, sq3, root3, gate, sq4, root4 = embedding(t - 1, P)
                out()
                first = {0: [sq3], 1: [root3]}
                second = {3: [gate], 4: [sq4], 6: [root4]}
            activations(t * HEADS, rows, first)
            activations(t * HEADS + 1, rows, second)
            with sc.Fori(2, HEADS) as h:
                activations(t * HEADS + h, rows)

        softmax_exp(0)
        tile(0, P, False)
        with sc.Fori(1, NT - 1) as t:
            tile(t, P, True)
        tile(NT - 1, TS, True)
        for step in embedding(NT - 1, TS):
            step()

    @block.vector
    def _(ve):
        own = Chain(ve, g.v_own)
        v = nc.vector

        def mean_root(dst, src, eps=EPS):
            own(v.tensor_scalar(dst, src, 1.0 / D, eps, ALU.mult, ALU.add))

        def exp_small(out, x, w):
            n, r, p = exs[:, 0, 0:w], exs[:, 1, 0:w], exs[:, 2, 0:w]
            own(v.tensor_scalar(n, x, 1.0 / math.log(2.0), MAGIC, ALU.mult, ALU.add))
            own(v.tensor_scalar(n, n, MAGIC, -126.0, ALU.subtract, ALU.max))
            own(v.tensor_scalar(n, n, 127.0, None, ALU.min))
            own(v.scalar_tensor_tensor(r, n, -0.693359375, x, ALU.mult, ALU.add))
            own(v.scalar_tensor_tensor(r, n, 2.12194440e-4, r, ALU.mult, ALU.add))
            own(v.tensor_scalar(p, r, 1.0 / 5040.0, None, ALU.mult))
            for c in (720.0, 120.0, 24.0, 6.0, 2.0, 1.0):
                own(v.scalar_tensor_tensor(p, p, 1.0 / c, r, ALU.add, ALU.mult))
            own(v.tensor_scalar(exi[:, 0:w], n, 127.0, 8388608.0, ALU.add, ALU.mult))
            own(v.scalar_tensor_tensor(out, p, 1.0, exi[:, 0:w].bitcast(F32), ALU.add, ALU.mult))

        def tt(out, x, y, op):
            own(v.tensor_tensor(out, x, y, op))

        ve.wait_ge(g.ss_ok, 1)
        own(v.memset(rstd[:], 1.0))
        own(v.tensor_scalar(rstd[:, 0:8], sumsq[:, 0:8], 1.0 / D, EPS, ALU.mult, ALU.add))
        v.tensor_scalar(rstd[0:TS, 8:9], sumsq[0:TS, 8:9], 1.0 / D, EPS, ALU.mult, ALU.add).then_inc(g.ms_ok, 1)
        ve.wait_ge(g.sq_ok, 1)
        own(v.reciprocal(rstd[:], rstd[:]))
        for t in range(NT):
            n = rows_of(t)
            v.tensor_scalar(xtok[0:n, t, :], xtok[0:n, t, :], rstd[0:n, t:t + 1], None, ALU.mult).then_inc(g.xn_ok, 1)
        ve.wait_ge(g.par_in, 16)
        for t in range(NT):
            n = rows_of(t)
            ve.wait_ge(g.xnT_tr, t + 1)
            ps = (psA, psB)[t % 2]
            for b in range(2):
                ins = v.tensor_tensor(xnT[:, 4 * b:4 * b + 4, P * t:P * t + n],
                                      ps[:, b, :].rearrange("p (k n) -> p k n", k=4)[:, :, 0:n],
                                      gmix[:, 4 * b:4 * b + 4].unsqueeze(2).broadcast_to([P, 4, n]), ALU.mult)
            ins.then_inc(g.xnT_ok, 1)
        q = s5s
        lr, li, ldt = q[:, 0], q[:, 1], q[:, 2]
        dt, mag, th = q[:, 3], q[:, 4], q[:, 5]
        rs, rc, sn, cs = q[:, 6], q[:, 7], q[:, 8], q[:, 9]
        t1, t2, t3 = q[:, 10], q[:, 11], q[:, 12]
        nr, den, cr, ci = q[:, 13], q[:, 14], q[:, 15], q[:, 16]
        ve.wait_ge(g.s5_in, 32)
        exp_small(dt, ldt, PAIRS)
        tt(t1, lr, dt, ALU.mult)
        exp_small(mag, t1, PAIRS)
        tt(th, li, dt, ALU.mult)
        C1, C2 = 6.28125, 0.00193500518798828125
        C3 = 2 * math.pi - C1 - C2
        for dst, quarter in ((rs, 0.0), (rc, 0.25)):
            own(v.tensor_scalar(t1, th, 1.0 / (2 * math.pi), quarter, ALU.mult, ALU.add))
            own(v.tensor_scalar(t1, t1, MAGIC, None, ALU.add))
            own(v.tensor_scalar(t1, t1, MAGIC, None, ALU.subtract))
            own(v.scalar_tensor_tensor(dst, t1, -C1, th, ALU.mult, ALU.add))
            own(v.scalar_tensor_tensor(dst, t1, -C2, dst, ALU.mult, ALU.add))
            own(v.scalar_tensor_tensor(dst, t1, -C3, dst, ALU.mult, ALU.add))
            own(v.tensor_scalar(dst, dst, quarter * 2 * math.pi, 3.1415925, ALU.add, ALU.min))
            own(v.tensor_scalar(dst, dst, -3.1415925, None, ALU.max))
        own(v.tensor_copy(t1, t1))
        v.tensor_copy(t2, t1).then_inc(g.s5_arg, 1)
        e, z, z2, pp = exs[:, 3, 0:8], exs[:, 4, 0:8], exs[:, 3, 8:16], exs[:, 4, 8:16]
        own(v.scalar_tensor_tensor(e, lam, -1.0, lam, ALU.mult, ALU.min))
        exp_small(z, e, 8)
        own(v.tensor_copy(e, z))
        own(v.tensor_scalar(z, e, 2.0, None, ALU.add))
        own(v.reciprocal(z, z))
        tt(z, z, e, ALU.mult)
        tt(z2, z, z, ALU.mult)
        own(v.tensor_scalar(pp, z2, 1.0 / 15.0, None, ALU.mult))
        for c in (13.0, 11.0, 9.0, 7.0, 5.0, 3.0):
            own(v.scalar_tensor_tensor(pp, pp, 1.0 / c, z2, ALU.add, ALU.mult))
        own(v.scalar_tensor_tensor(z, pp, 1.0, z, ALU.add, ALU.mult))
        own(v.tensor_scalar(e, lam, -1.0, 0.0, ALU.mult, ALU.max))
        own(v.scalar_tensor_tensor(z, z, 2.0, e, ALU.mult, ALU.add))
        own(v.tensor_scalar(spk[:], z, -4.0, None, ALU.mult))
        ve.wait_ge(g.s5_act, 1)
        own(v.memset(pw[:, 0, :, 0], 1.0))
        own(v.memset(pw[:, 1, :, 0], 0.0))
        tt(pw[:, 0, :, 1], mag, cs, ALU.mult)
        tt(pw[:, 1, :, 1], mag, sn, ALU.mult)
        ar, ai = pw[:, 0, :, 1], pw[:, 1, :, 1]
        for n in range(2, STEP + 1):
            pr, pi = pw[:, 0, :, n - 1], pw[:, 1, :, n - 1]
            tt(t1, pr, ar, ALU.mult)
            tt(t2, pi, ai, ALU.mult)
            tt(pw[:, 0, :, n], t1, t2, ALU.subtract)
            tt(t1, pr, ai, ALU.mult)
            tt(t2, pi, ar, ALU.mult)
            tt(pw[:, 1, :, n], t1, t2, ALU.add)
        own(v.tensor_copy(pwr[:], pw[:, :, :, STEP - 1::-1]))
        own(v.tensor_copy(A8[:, 0, 0], pw[:, 0, :, STEP]))
        own(v.tensor_scalar(A8[:, 0, 1], pw[:, 1, :, STEP], -1.0, None, ALU.mult))
        own(v.tensor_copy(A8[:, 1, 0], pw[:, 1, :, STEP]))
        own(v.tensor_copy(A8[:, 1, 1], pw[:, 0, :, STEP]))
        own(v.tensor_scalar(nr, ar, -1.0, None, ALU.add))
        tt(t1, lr, lr, ALU.mult)
        tt(t2, li, li, ALU.mult)
        tt(den, t1, t2, ALU.add)
        own(v.reciprocal(den, den))
        tt(t1, nr, lr, ALU.mult)
        tt(t2, ai, li, ALU.mult)
        tt(t1, t1, t2, ALU.add)
        tt(cr, t1, den, ALU.mult)
        tt(t1, ai, lr, ALU.mult)
        tt(t2, nr, li, ALU.mult)
        tt(t1, t1, t2, ALU.subtract)
        tt(ci, t1, den, ALU.mult)
        crb, cib = (x.unsqueeze(2).broadcast_to([P, PAIRS, GC]) for x in (cr, ci))
        tb = tmpb[:, 0:PAIRS * GC].rearrange("p (g c) -> p g c", g=PAIRS)
        tt(bb[:, 0], s5w[:, 0], crb, ALU.mult)
        tt(tb, s5w[:, 1], cib, ALU.mult)
        tt(bb[:, 0], bb[:, 0], tb, ALU.subtract)
        tt(bb[:, 1], s5w[:, 1], crb, ALU.mult)
        tt(tb, s5w[:, 0], cib, ALU.mult)
        tt(bb[:, 1], bb[:, 1], tb, ALU.add)

        def spread(out, x, y, n, op):
            tt(out, x.unsqueeze(3).broadcast_to([P, PAIRS, n, GC]), y.unsqueeze(2).broadcast_to([P, PAIRS, n, GC]), op)
        tm = tmpb[:, 0:PAIRS * STEP * GC].rearrange("p (g n c) -> p g n c", g=PAIRS, n=STEP)
        spread(M1T[:, :, 0], pwr[:, 0], bb[:, 0], STEP, ALU.mult)
        spread(tm, pwr[:, 1], bb[:, 1], STEP, ALU.mult)
        tt(M1T[:, :, 0], M1T[:, :, 0], tm, ALU.subtract)
        spread(M1T[:, :, 1], pwr[:, 0], bb[:, 1], STEP, ALU.mult)
        spread(tm, pwr[:, 1], bb[:, 0], STEP, ALU.mult)
        v.tensor_tensor(M1T[:, :, 1], M1T[:, :, 1], tm, ALU.add).then_inc(g.s5_ready, 1)
        ve.wait_ge(g.s5_ready, 1)
        tm = tmpb[:, :].rearrange("p (g n c) -> p g n c", g=PAIRS, n=STEP + 1)
        spread(CX[:, :, 0], pw[:, 0], s5w[:, 2], STEP + 1, ALU.mult)
        spread(tm, pw[:, 1], s5w[:, 3], STEP + 1, ALU.mult)
        tt(CX[:, :, 0], CX[:, :, 0], tm, ALU.subtract)
        spread(CX[:, :, 1], pw[:, 0], s5w[:, 3], STEP + 1, ALU.mult)
        spread(tm, pw[:, 1], s5w[:, 2], STEP + 1, ALU.mult)
        for n in range(0, STEP + 1, 3):
            own(v.scalar_tensor_tensor(CX[:, :, 1, n:n + 3].rearrange("p g n c -> p g (n c)"),
                                       CX[:, :, 1, n:n + 3].rearrange("p g n c -> p g (n c)"), -1.0,
                                       tm[:, :, n:n + 3].rearrange("p g n c -> p g (n c)"), ALU.mult, ALU.subtract))
        v.tensor_copy(t2, t1).then_inc(g.s5_ready, 1)
        ve.wait_ge(g.dbc_in, 16)
        ve.wait_ge(g.ut_tr, 9)
        dgc = dbc[:].rearrange("p (g c) -> p g c", g=NG).unsqueeze(2)
        own(v.tensor_tensor(u_c[:], u_c[:], dgc.broadcast_to([P, NG, STEP, GC]), ALU.mult))
        own(v.tensor_tensor(u_s[:], u_s[:], dgc[0:SB].broadcast_to([SB, NG, STEP, GC]), ALU.mult))
        ve.wait_ge(g.m1_tr, 8)
        own(v.memset(V[:, 0], 0.0))
        for b in range(PAIRS):
            ve.wait_ge(g.v_mm, b + 1)
            src = psC[:, b % 2, :].rearrange("p (r n) -> p n r", r=2)
            own(v.tensor_copy(V[:, 1:NB + 1, :, b], src[:, 0:NB]))
            v.tensor_copy(V[:, NB + 1 + SB:SLOTS, :, b], src[:, NB:NB + SB]).then_inc(g.v_ok, 1)
        own(v.tensor_copy(t2, t1))
        v.tensor_copy(t2, t1).then_inc(g.v_ok, 1)

        def add_to_u(mm, done):
            for b in range(8):
                for w, (ps, buf, n) in enumerate(((psA, u_c, NB), (psB, u_s, SB))):
                    ve.wait_ge(mm, 2 * b + w + 1)
                    view = buf[:, groups(b)].rearrange("p q j c -> p q (j c)")
                    v.tensor_tensor(view, view, ps[0:n, b % 2, :].rearrange("p (q n) -> p q n", q=4),
                                    ALU.add).then_inc(done, 1)
        add_to_u(g.y1_mm, g.y1_ok)

        ve.wait_ge(g.y1_mm, 16)
        own(v.memset(xpad[:, 0:3], 0.0))
        with ve.Fori(0, KD) as h:
            PER = 23
            own.enter(h * PER)
            own(v.tensor_copy(hpar[:, 0:7], lrup[:, bass.ds(h, 1), :].rearrange("p a n -> p (a n)")))
            v.tensor_copy(hpar[:, 7:8], spk[:, bass.ds(h, 1)]).then_inc(g.hcol_ok, 1)
            ve.wait_ge(g.hcol_ok, h + 1)
            own(v.tensor_copy(xpads[:, :, 0:3], cst[:, bass.ds(h, 1)].rearrange("p a b n -> p (a b) n")))
            ve.wait_ge(g.xb_ok, h + 1)
            xcs = xc[:, TP:T].rearrange("p (b l) -> p b l", b=SB)
            own(v.tensor_scalar(xc[:, 0:TP], xpad[:, 0:TP], hpar[:, 0:1], hpar[:, 4:5], ALU.mult, ALU.add))
            own(v.tensor_scalar(xcs, xpads[:, :, 0:SL], hpar[:, 0:1], hpar[:, 4:5], ALU.mult, ALU.add))
            own(v.tensor_copy(nconv[:, bass.ds(h, 1), 0].rearrange("p a n -> p (a n)"), xpad[:, TP:TP + 3]))
            own(v.tensor_copy(nconv[:, bass.ds(h, 1), 1:].rearrange("p a b n -> p (a b) n"), xpads[:, :, SL:SL + 3]))
            for k in range(1, 4):
                own(v.scalar_tensor_tensor(xcs, xpads[:, :, k:k + SL], hpar[:, k:k + 1], xcs, ALU.mult, ALU.add))
                ins = v.scalar_tensor_tensor(xc[:, 0:TP], xpad[:, k:k + TP], hpar[:, k:k + 1], xc[:, 0:TP],
                                             ALU.mult, ALU.add)
                if k < 3:
                    own(ins)
            ins.then_inc(g.conv_ok, 1)
            ve.wait_ge(g.conv_ok, h + 1)
            ve.wait_ge(g.tanh_ok, h + 1)
            own(v.tensor_scalar(dn[:], rt[:], -1.0, 1.0, ALU.mult, ALU.add))
            own(v.reciprocal(dn[:], dn[:]))
            v.scalar_tensor_tensor(av[:], rt[:], 1.0, dn[:], ALU.add, ALU.mult).then_inc(g.den_ok, 1)
            own(v.tensor_tensor(ig[:], ig[:], xc[:], ALU.mult))
            own(v.tensor_tensor(ig[:], ig[:], dn[:], ALU.mult))
            ve.wait_ge(g.den_ok, h + 1)
            ve.wait_ge(g.sqrt_ok, h + 1)
            own(v.tensor_tensor(ig[:], ig[:], rt[:], ALU.mult))
            start_a = av[:, TP:T].rearrange("p (b l) -> p b l", b=SB)[:, :, 0]
            start_b = ig[:, TP:T].rearrange("p (b l) -> p b l", b=SB)[:, :, 0]
            own(v.tensor_tensor(exs[:, 0, 0:SB], start_a, h0[:, bass.ds(h, 1)].rearrange("p a b -> p (a b)"), ALU.mult))
            own(v.tensor_tensor(start_b, start_b, exs[:, 0, 0:SB], ALU.add))
            own(v.memset(start_a, 0.0))
            own(v.tensor_tensor_scan(dn[:], av[:], ig[:], 0.0, ALU.mult, ALU.add))
            own(v.tensor_copy(nlru[:, bass.ds(h, 1), 0:1].rearrange("p a n -> p (a n)"), dn[:, TP - 1:TP]))
            own(v.tensor_copy(nlru[:, bass.ds(h, 1), 1:].rearrange("p a n -> p (a n)"), dn[:, TP + SL - 1:T:SL]))
            ve.wait_ge(g.gb_ok, h + 1)
            own(v.tensor_copy(hpar[:, 7:8], hpar[:, 7:8]))
            v.tensor_tensor(ybT[:, bass.ds(h, 1), :].rearrange("p a n -> p (a n)"), gg[:], dn[:],
                            ALU.mult).then_inc(g.yb_ok, 1)
            ve.wait_ge(g.yb_ok, h + 1)
        own.leave(KD, PER)
        add_to_u(g.y2_mm, g.y2_ok)
        ve.wait_ge(g.sig_ok, 4)
        own(v.tensor_tensor(yaT[:, 0:2], yaT[:, 0:2], sig[:, 0:2], ALU.mult))
        v.tensor_tensor(yaT[:, 2:4], yaT[:, 2:4], sig[:, 2:4], ALU.mult).then_inc(g.ya_done, 1)
        own(v.tensor_copy(hpar[:, 7:8], hpar[:, 7:8]))
        v.tensor_copy(hpar[:, 7:8], hpar[:, 7:8]).then_inc(g.mg_ok, 1)
        with ve.Fori(0, KD) as m:
            ve.wait_ge(g.sga_ok, m + 1)
            ve.wait_ge(g.ya_mm, m + 1)
            for c, (o, n) in enumerate(CHUNKS):
                ins = v.tensor_tensor(mg[:, o:o + n], psB[:, c, 0:n], sga[:, o:o + n], ALU.mult)
            ins.then_inc(g.mga_ok, 1)
            ve.wait_ge(g.sgb_ok, m + 1)
            ve.wait_ge(g.yb_mm, m + 1)
            own.enter(m)
            for c, (o, n) in enumerate(CHUNKS):
                ins = v.tensor_tensor(sgb[:, o:o + n], psB[:, c, 0:n], sgb[:, o:o + n], ALU.mult)
            own(ins)
            ve.wait_ge(g.mga_ok, m + 1)
            v.tensor_tensor(mgT[:, bass.ds(m, 1), :].rearrange("p a n -> p (a n)"), mg[:], sgb[:],
                            ALU.add).then_inc(g.mg_ok, 1)
        own.leave(KD, 1)
        ve.wait_ge(g.gffn_in, 16)
        for t in range(NT):
            n = rows_of(t)
            ps = (psC, psB)[t % 2]
            ve.wait_ge(g.o_mm, t + 1)
            ve.wait_ge(sem(f"xr_in{t % 2}"), 16 * (t // 2 + 1))
            v.tensor_tensor(x2[0:n, t, :], xr[0:n, t % 2, :], ps[0:n, 0:2, :].rearrange("p a n -> p (a n)"),
                            ALU.add).then_inc(g.x2_ok, 1)
            ve.wait_ge(g.ss2_ok, t + 1)
            v.tensor_scalar(rstd2[0:n, t:t + 1], sumsq2[0:n, t:t + 1], 1.0 / D, EPS, ALU.mult,
                            ALU.add).then_inc(g.ms2_ok, 1)
            ve.wait_ge(g.sq2_ok, t + 1)
            own(v.reciprocal(rstd2[0:n, t:t + 1], rstd2[0:n, t:t + 1]))
            v.scalar_tensor_tensor(xn2s[0:n, t % 2, :], x2[0:n, t, :], rstd2[0:n, t:t + 1], gffn[0:n, :],
                                   ALU.mult, ALU.mult).then_inc(g.xn2_ok, 1)
        ve.wait_ge(g.g_sv, 2)
        ve.wait_ge(g.o_mm, NT)
        v.tensor_copy(hpar[:, 7:8], hpar[:, 7:8]).then_inc(g.top_ok, 1)
        with ve.Fori(0, HEADS) as h:
            per = 2 * 4 * NT + 3
            own.enter(h * per)
            for s in range(2):
                ve.wait_ge(g.sc_mm, h * 2 + (s + 1))
                for t in range(NT):
                    n = rows_of(t)
                    score = psB[0:n, t // 4, P * (t % 4):P * (t % 4 + 1)]
                    lo, hi = svh[0:n, t, s, 0:8], svh[0:n, t, s, 8:16]
                    alone(ve)
                    own(v.max(lo, score))
                    alone(ve)
                    own(v.match_replace(srep[0:n, 0, :], lo, score, BELOW))
                    alone(ve)
                    own(v.max(hi, srep[0:n, 0, :]))
                    alone(ve)
                    v.max_index(sih[0:n, t, s, 0:8], lo, score)
                    own(v.max_index(sih[0:n, t, s, 8:16], hi, srep[0:n, 0, :]))
                v.tensor_copy(exs[:, 0, 0:1], exs[:, 0, 0:1]).then_inc(g.top_ok, 1)
            for dst, src in ((sv, svh), (si, sih)):
                view = dst[:, 0:UNITS].rearrange("p (t h) s n -> p t h (s n)", h=HEADS)
                view = view[:, :, bass.ds(h, 1)].rearrange("p t a n -> p t (a n)")
                v.tensor_copy(view[:, 0:NT - 1], src[:, 0:NT - 1].rearrange("p t s n -> p t (s n)"))
                own(v.tensor_copy(view[0:TS, NT - 1:NT], src[0:TS, NT - 1:NT].rearrange("p t s n -> p t (s n)")))
            own(v.tensor_copy(exs[:, 0, 0:1], exs[:, 0, 0:1]))
        own.leave(HEADS, per)
        ve.wait_ge(g.sc_mm, 2 * HEADS)
        v.tensor_copy(exs[:, 0, 0:1], exs[:, 0, 0:1]).then_inc(g.q_done, 1)

        own_g = Chain(ve, g.v_g)

        def choose(u, s):
            def half(buf, i):
                return buf[:, bass.ds(u, 1), i].rearrange("p a n -> p (a n)")
            own_g(v.tensor_tensor(cand[:], half(sv, 0).unsqueeze(2).broadcast_to([P, TOPK, TOPK]),
                                  half(sv, 1).unsqueeze(1).broadcast_to([P, TOPK, TOPK]), ALU.add))
            alone(ve)
            own_g(v.max(top[:, 0:8], cand[:]))
            alone(ve)
            own_g(v.match_replace(crep[:], top[:, 0:8], cand[:], BELOW))
            alone(ve)
            own_g(v.max(top[:, 8:16], crep[:]))
            own_g(v.tensor_scalar(gate_sum[:, 0:1], top[:, 0:1], -1.0, None, ALU.mult))
            v.tensor_copy(gate_sum[:, 2:3], top[:, 0:1]).then_inc(g.l2_top, 1)
            cf, rf = cand[:].rearrange("p a b -> p (a b)"), crep[:].rearrange("p a b -> p (a b)")
            v.max_index(pos[:, 0:8], top[:, 0:8], cf)
            own_g(v.max_index(pos[:, 8:16], top[:, 8:16], rf))
            v.tensor_scalar(pab[:, 0], pos[:], 4, None, ALU.logical_shift_right)
            own_g(v.tensor_scalar(pab[:, 1], pos[:], 15, None, ALU.bitwise_and))
            own_g(v.tensor_copy(pabf[:], pab[:]))
            own_g(v.tensor_tensor(hot[:], pabf[:].unsqueeze(3).broadcast_to([P, 2, TOPK, TOPK]),
                                  iota[:].unsqueeze(1).unsqueeze(1).broadcast_to([P, 2, TOPK, TOPK]), ALU.is_equal))
            own_g(v.tensor_tensor(hot[:], hot[:], si[:, bass.ds(u, 1)].rearrange("p a s n -> p (a s) n").unsqueeze(2)
                                  .broadcast_to([P, 2, TOPK, TOPK]), ALU.mult))
            own_g(v.tensor_reduce(pick[:], hot[:], AX.X, ALU.add))
            v.scalar_tensor_tensor(idxu[:, s], pick[:, 0], float(NKEY), pick[:, 1], ALU.mult,
                                   ALU.add).then_inc(g.idx_ok, 1)

        def weigh(u, s):
            ve.wait_ge(g.l2_exp, u + 1)
            own_g(v.reciprocal(gate_sum[:, 2:3], gate_sum[:, 1:2]))
            own_g(v.tensor_scalar(gw[:, s], expt[:], gate_sum[:, 2:3], None, ALU.mult))
            own_g(v.tensor_copy(gate_sum[:, 2:3], gate_sum[:, 1:2]))

        def diagonals(u, s, q, rows):
            ve.wait_ge(g.act_ok, u * 8 + (q + 1))
            for k in (2 * q, 2 * q + 1):
                ve.wait_ge(g.slot_free, u * TOPK + (k + RING - 3))
                v.tensor_scalar(dg[0:rows, k % 4, 0:rows], ident[0:rows, 0:rows], act[0:rows, k:k + 1],
                                gw[0:rows, s, k:k + 1], ALU.mult, ALU.mult).then_inc(g.diag_ok, 1)

        def unit(u, s, rows, between={}):
            for q in range(TOPK // 2):
                for k in (2 * q, 2 * q + 1):
                    r = k % RING
                    ve.wait_ge(gathered[r], u * 32 + 16 * (k // RING + 1))
                    ins = v.tensor_tensor_reduce(ring[0:rows, r, 0:D], ring[0:rows, r, 0:D], xn2c[0:rows, :], 1.0, 0.0,
                                                 ALU.mult, ALU.add, dot[0:rows, k:k + 1])
                ins.then_inc(g.dot_ok, 1)
                if q >= 1:
                    diagonals(u, s, q - 1, rows)
                if q == 0:
                    choose(u + 1, 1 - s)
                if q == 2:
                    weigh(u + 1, 1 - s)
                for step in between.get(q, ()):
                    step()
            diagonals(u, s, TOPK // 2 - 1, rows)

        own_e = Chain(ve, g.v_tail)

        def embedding(t, rows):
            def mean(ready, done):
                def run():
                    ve.wait_ge(ready, t + 1)
                    v.tensor_scalar(tail_s[0:rows, 1:2], tail_s[0:rows, 0:1], 1.0 / D, EPS, ALU.mult,
                                    ALU.add).then_inc(done, 1)
                return run

            def normed():
                ve.wait_ge(g.sq3_ok, t + 1)
                own_e(v.reciprocal(tail_s[0:rows, 2:3], tail_s[0:rows, 1:2]))
                v.tensor_scalar(xn3[0:rows, :], x3[0:rows, :], tail_s[0:rows, 2:3], None, ALU.mult).then_inc(g.xn3_ok, 1)

            def gain():
                ve.wait_ge(g.xn3_tr, t + 1)
                for b in range(2):
                    ins = v.tensor_tensor(xn3T[:, 4 * b:4 * b + 4, 0:rows],
                                          psA[:, b, :].rearrange("p (k n) -> p k n", k=4)[:, :, 0:rows],
                                          gple[:, 4 * b:4 * b + 4].unsqueeze(2).broadcast_to([P, 4, rows]), ALU.mult)
                ins.then_inc(g.xn3T_ok, 1)

            def gated():
                ve.wait_ge(g.gate3_ok, t + 1)
                own_e(v.tensor_tensor(xn3[0:rows, :], xn3[0:rows, :],
                                      psA[0:rows, 0:2, :].rearrange("p a n -> p (a n)"), ALU.mult))
                v.tensor_tensor(x3[0:rows, :], x3[0:rows, :], xn3[0:rows, :], ALU.add).then_inc(g.x4_ok, 1)

            def final():
                ve.wait_ge(g.sq4_ok, t + 1)
                own_e(v.reciprocal(tail_s[0:rows, 2:3], tail_s[0:rows, 1:2]))
                v.scalar_tensor_tensor(xn3[0:rows, :], x3[0:rows, :], tail_s[0:rows, 2:3], gfin[0:rows, :], ALU.mult,
                                       ALU.mult).then_inc(g.y_ok, 1)
            return mean(g.ss3_ok, g.ms3_ok), normed, gain, gated, mean(g.ss4_ok, g.ms4_ok), final

        def tile(t, rows, before):
            own_g(v.scalar_tensor_tensor(xn2c[0:rows, :], x2[0:rows, bass.ds(t, 1), :].rearrange("p a n -> p (a n)"),
                                         rstd2[0:rows, bass.ds(t, 1)], gffn[0:rows, :], ALU.mult, ALU.mult))
            first, second = {}, {}
            if before:
                mean3, normed, gain, gated, mean4, final = embedding(t - 1, P)
                first = {0: [mean3], 2: [normed], 4: [gain]}
                second = {4: [gated], 5: [mean4], 7: [final]}
            unit(t * HEADS, 0, rows, first)
            unit(t * HEADS + 1, 1, rows, second)
            alone(ve)
            with ve.Fori(1, HEADS // 2) as w:
                own_g.enter((w - 1) * (2 * per_unit))
                for s in range(2):
                    unit(t * HEADS + w * 2 + s, s, rows)
            own_g.leave(HEADS // 2 - 1, 2 * per_unit)

        choose(0, 0)
        weigh(0, 0)
        per_unit = own_g.done
        per_tile = 1 + HEADS * per_unit
        ve.wait_ge(g.y_out, 16)
        tile(0, P, False)
        with ve.Fori(1, NT - 1) as t:
            own_g.enter((t - 1) * per_tile)
            own_e.enter((t - 1) * 3)
            tile(t, P, True)
        own_g.leave(NT - 2, per_tile)
        own_e.leave(NT - 2, 3)
        tile(NT - 1, TS, True)
        for step in embedding(NT - 1, TS):
            step()

    ctx.close()


_OUT = {
    "o_y": (T, D), "o_s5": (P, 1 + SB, 2, PAIRS), "o_lru": (P, KD, 1 + SB), "o_conv": (P, KD, 1 + SB, 3),
}


def layout(inp):
    import numpy as np
    i = {k: np.asarray(x) for k, x in inp.items()}

    def cols(x):
        return x.reshape(-1, P).T

    def blocks(w):
        k, n = w.shape
        return np.ascontiguousarray(w.reshape(k // P, P, n // P, P).transpose(2, 1, 0, 3))

    def rows(w):
        return np.ascontiguousarray(w.reshape(-1, P, w.shape[1]).transpose(1, 0, 2))

    def state(x):
        x = x.reshape((PAIRS, 2, NS) + x.shape[2:])
        return np.moveaxis(x, 0, 2).reshape((P, PAIRS) + x.shape[3:])

    win = i["w_in"][0]
    o = {}
    o["x"] = np.concatenate([i["x_prompt"][0], i["x_sample"].reshape(TS, D)], axis=0)
    lru = np.stack([cols(i["conv_w"][0, k]) for k in range(4)]
                   + [cols(i[n][0]) for n in ("conv_b", "lru_b_r", "lru_b_i")], axis=2)
    o["par"] = np.concatenate([
        cols(i["g_mix"][0]), cols(i["g_ple"][0]), cols(i["s5_b_glu"][0]), cols(i["lru_lam"][0]),
        lru.reshape(P, -1), i["state_lru"][0].reshape(SB, KD, P).transpose(2, 1, 0).reshape(P, -1),
        i["state_conv"][0].reshape(SB, 3, KD, P).transpose(3, 2, 0, 1).reshape(P, -1)], axis=1)
    ldt = np.broadcast_to(i["s5_log_dt"][0][:, None], (NG, NS))
    o["s5_small"] = np.stack([state(i["s5_lam_re"][0]), state(i["s5_lam_im"][0]), state(ldt)], axis=1)
    o["s5_w"] = np.stack([state(i["s5_b_re"][0]), state(i["s5_b_im"][0]),
                          state(i["s5_c_re"][0].transpose(0, 2, 1)), state(i["s5_c_im"][0].transpose(0, 2, 1))], axis=1)
    o["s5_d"] = i["s5_d"][0]
    h = [np.moveaxis(np.stack([state(x[b]) for b in range(SB)], axis=1), 1, 1)
         for x in (i["state_s5_re"][0], i["state_s5_im"][0])]
    o["h_s5"] = np.stack(h, axis=2)
    o["w_xa"] = rows(win[:, 0:S5W])
    wb = blocks(win[:, S5W:])
    o["w_xb"], o["w_gb"], o["w_ga"], o["w_gp"] = wb[0:8], wb[8:16], wb[16:24], wb[24:32]
    o["w_ri"] = np.stack([i["lru_w_r"][0], i["lru_w_i"][0]], axis=2)
    o["w_glu"] = rows(i["s5_w_glu"][0])
    o["w_ya"], o["w_yb"] = blocks(i["w_a_proj"][0]), blocks(i["w_b_proj"][0])
    o["w_out"] = rows(i["w_out"][0])
    o["g_ffn"], o["g_final"] = i["g_ffn"][0], i["g_final"]
    o["keys"] = i["peer_sub_keys"][0].reshape(2 * HEADS, NKEY, P).transpose(2, 0, 1)
    o["w_q"] = blocks(i["peer_w_q"][0])
    o["uv"] = np.concatenate([i["peer_u"][0], i["peer_v"][0]], axis=1)
    o["w_gate"], o["w_ple"] = rows(i["w_ple_gate"][0]), rows(i["w_ple"][0])
    p = np.concatenate([i["p_prompt"][0, 0], i["p_sample"][0].reshape(TS, -1)], axis=0)
    o["p_T"] = p.T.reshape(2, P, T).transpose(1, 0, 2)
    return {k: np.ascontiguousarray(x) for k, x in o.items()}


def program(nc, arrays):
    a = {n: nc.dram_tensor("in_" + n, x.shape, F32, kind="ExternalInput").ap() for n, x in arrays.items()}
    a.update({n: nc.dram_tensor(n, s, F32, kind="ExternalOutput").ap() for n, s in _OUT.items()})
    a["scr"] = nc.dram_tensor("scr", (TS, S5W), F32).ap()
    build(nc, a)


def kernel(**inputs):
    import numpy as np
    import concourse.bacc as bacc
    from concourse.bass_utils import run_bass_kernel_spmd
    arrays = layout(inputs)
    nc = bacc.Bacc("TRN2", target_bir_lowering=False, num_devices=1)
    program(nc, arrays)
    r = run_bass_kernel_spmd(nc, [{"in_" + n: x for n, x in arrays.items()}], core_ids=[0]).results[0]
    y = np.asarray(r["o_y"])
    s5 = np.asarray(r["o_s5"]).reshape(2, NS, 1 + SB, 2, PAIRS).transpose(3, 2, 4, 0, 1).reshape(2, 1 + SB, NG, NS)
    lru = np.asarray(r["o_lru"]).transpose(2, 1, 0).reshape(1 + SB, D)
    conv = np.asarray(r["o_conv"]).transpose(2, 3, 1, 0).reshape(1 + SB, 3, D)
    c = np.ascontiguousarray
    return (c(y[0:TP].reshape(1, TP, D)), c(y[TP:].reshape(SB, SL, D)),
            c(s5[0, 0:1][None]), c(s5[1, 0:1][None]), c(lru[0:1][None]), c(conv[0:1][None]),
            c(s5[0, 1:][None]), c(s5[1, 1:][None]), c(lru[1:][None]), c(conv[1:][None]))
```

```python
import math
from contextlib import ExitStack

import concourse.bass as bass
from concourse import mybir

F32 = mybir.dt.float32
I32 = mybir.dt.int32
U32 = mybir.dt.uint32
ALU = mybir.AluOpType
ACT = mybir.ActivationFunctionType
AX = mybir.AxisListType

P = 128
D = 1024
KD = D // P
TP, TS = 1024, 64
T = TP + TS
SB, SL = 8, 8
NT = 9
CHUNKS = [(0, 384), (384, 384), (768, 320)]
S5W, NG, GC, NS = 512, 32, 16, 64
PAIRS = NG // 2
STEP = 8
NB = TP // STEP
SLOTS = NB + 1 + 2 * SB
HEADS, TOPK, NKEY = 8, 16, 128
RING = 8
EPS = 1e-6
MAGIC = 12582912.0
LOADS = [(0, 2), (2, 5), (5, 8), (8, 9)]
BELOW = -3.0e38
UNITS = NT * HEADS
XA_FIRST = 6


def group_of(batch, q):
    return 8 * (batch // 2) + 2 * q + batch % 2


def groups(batch):
    return slice(group_of(batch, 0), group_of(batch, 3) + 1, 2)


def rows_of(t):
    return P if t < NT - 1 else TS


class Chain:

    def __init__(self, eng, sem):
        self.eng, self.sem, self.done, self.shift, self.outer = eng, sem, 0, 0, []

    def __call__(self, ins):
        ins.then_inc(self.sem, 1)
        self.done += 1
        self.eng.wait_ge(self.sem, self.shift + self.done)

    def enter(self, shift):
        self.outer.append((self.shift, self.done))
        self.shift = self.shift + shift

    def leave(self, trips, per):
        self.shift, start = self.outer.pop()
        assert self.done - start == per, (self.done - start, per)
        self.done = start + trips * per


def build(nc, a):
    ctx = ExitStack()
    base = (nc.sbuf_base + 31) // 32 * 32
    SMALL, XNT = base, base + 14336
    YAT = XNT + 34816
    R1 = YAT + 17408
    VREG = R1 + 34816
    CXR = VREG + 18560
    UC = CXR + 18432
    US = UC + 16384
    R2 = US + 16384
    END = nc.sbuf_usable_end

    def region(start, end):
        at = [start]

        def put(name, shape, dt=F32):
            n = 4
            for s in shape[1:]:
                n *= s
            t = nc.alloc_sbuf_tensor_at(name, shape, dt, offset=at[0])
            at[0] += (n + 31) // 32 * 32
            assert at[0] <= end, (name, at[0] - end)
            return t
        return put

    put = region(SMALL, XNT)
    ident = put("ident", [P, P])
    par = put("par", [P, 340])
    nconv = put("nconv", [P, KD, 1 + SB, 3])
    nlru = put("nlru", [P, KD, 1 + SB])
    sumsq = put("sumsq", [P, NT])
    rstd = put("rstd", [P, NT])
    sumsq2 = put("sumsq2", [P, NT])
    rstd2 = put("rstd2", [P, NT])
    spk = put("spk", [P, KD])
    hpar = put("hpar", [P, 8])
    A8 = put("A8", [P, 2, 2, PAIRS])
    cp_t = put("cp_t", [P, 2, 2, PAIRS])
    cp_u = put("cp_u", [P, 2, PAIRS])
    cs_t = put("cs_t", [P, SB, 2, PAIRS])
    dbc = put("dbc", [P, S5W])
    exs = put("exs", [P, 5, PAIRS])
    exi = put("exi", [P, PAIRS], I32)
    iota = put("iota", [P, TOPK])
    idxu = put("idxu", [P, 2, TOPK], U32)
    gw = put("gw", [P, 2, TOPK])
    dot = put("dot", [P, TOPK])
    act = put("act", [P, TOPK])
    gate_sum = put("gate_sum", [P, 4])
    top = put("top", [P, TOPK])
    pos = put("pos", [P, TOPK], U32)
    pab = put("pab", [P, 2, TOPK], U32)
    pabf = put("pabf", [P, 2, TOPK])
    pick = put("pick", [P, 2, TOPK])
    expt = put("expt", [P, TOPK])
    tail_s = put("tail_s", [P, 4])
    gmix, gple = par[:, 0:8], par[:, 8:16]
    bglu, lam = par[:, 16:20], par[:, 20:28]
    lrup = par[:, 28:84].rearrange("p (h n) -> p h n", h=KD)
    h0 = par[:, 84:148].rearrange("p (h b) -> p h b", h=KD)
    cst = par[:, 148:340].rearrange("p (h b n) -> p h b n", h=KD, b=SB)

    xnT = region(XNT, YAT)("xnT", [P, KD, T])
    xtok = region(YAT, VREG)("xtok", [P, NT, D])
    yaT = region(YAT, R1)("yaT", [P, 4, T])
    put = region(YAT, R1)
    Ksb = put("Ksb", [GC, NG, P])
    put = region(YAT, R1)
    y2st = put("y2st", [P, 4, 4 * P])
    y2st_s = put("y2st_s", [SB, 4, 4 * P])
    ybT = region(R1, VREG)("ybT", [P, KD, T])
    put = region(R1, VREG)
    M1 = put("M1", [P, NG, P])
    uT = put("uT", [P, NG, NB + SB])
    V = region(VREG, CXR)("V", [P, SLOTS, 2, PAIRS])
    M1T = region(VREG, CXR)("M1T", [P, PAIRS, 2, STEP, GC])
    sig = region(UC, R2 - 8192)("sig", [P, 4, T])
    CX = region(CXR, UC)("CX", [P, PAIRS, 2, STEP + 1, GC])
    u_c = region(UC, US)("u_c", [P, NG, STEP, GC])
    u_s = region(US, R2)("u_s", [SB, NG, STEP, GC])
    put = region(US, R2)
    tmpb = put("tmpb", [P, PAIRS * (STEP + 1) * GC])
    s5w = put("s5w", [P, 4, PAIRS, GC])
    bb = put("bb", [P, 2, PAIRS, GC])
    put = region(R2, END)
    M3 = put("M3", [P, NG, P])
    wxa = put("wxa", [P, KD, S5W])
    ust = put("ust", [TS, S5W])
    s5s = put("s5s", [P, 24, PAIRS])
    pw = put("pw", [P, 2, PAIRS, STEP + 1])
    pwr = put("pwr", [P, 2, PAIRS, STEP])
    dk = put("dk", [GC, NG, GC])
    put = region(R2, END)
    w_xb = put("w_xb", [P, KD, P])
    w_gb = put("w_gb", [P, KD, P])
    w_ri = put("w_ri", [P, 2, P])
    xpad = put("xpad", [P, 3 + TP])
    xpads = put("xpads", [P, SB, 3 + SL])
    xc, rt, ig, av, dn, gg = (put(n, [P, T]) for n in ("xc", "rt", "ig", "av", "dn", "gg"))
    y_c = region(VREG, CXR)("y_c", [P, STEP, S5W])
    y_s = region(CXR, UC)("y_s", [SB, STEP, S5W])
    wglu = region(R2 - 8192, R2)("wglu", [P, 4, S5W])
    put = region(R2, END)
    w_ga = put("w_ga", [P, KD, P])
    w_gp = put("w_gp", [P, KD, P])
    w_ya = put("w_ya", [P, 4, P])
    w_yb = put("w_yb", [P, KD, P])
    sga, sgb, mg = (put(n, [P, T]) for n in ("sga", "sgb", "mg"))
    mgT = region(VREG, UC)("mgT", [P, KD, T])
    wout = region(UC, R2)("wout", [P, KD, D])
    x2 = region(XNT, R1)("x2", [P, NT, D])
    xn2T = region(R1, VREG)("xn2T", [P, KD, T])
    put = region(R2, END)
    gffn = put("gffn", [P, D])
    sv = put("sv", [P, UNITS + 1, 2, TOPK])
    si = put("si", [P, UNITS + 1, 2, TOPK])
    xr = put("xr", [P, 2, D])
    xn2s = put("xn2s", [P, 2, D])
    RNG = XNT + 36864
    w_q = region(RNG, R1)("w_q", [P, 2, KD, P])
    put = region(VREG, RNG + 65536 + 1536)
    keys = put("keys", [P, 2 * HEADS, NKEY])
    qT = put("qT", [P, 2, T])
    put = region(RNG + 65536 + 9728, R2)
    wgate = put("wgate", [P, KD, D])
    wple = put("wple", [P, 2, D])
    svh = put("svh", [P, NT, 2, TOPK])
    sih = put("sih", [P, NT, 2, TOPK], U32)
    put = region(RNG, RNG + 65536 + 1024)
    ring = put("ring", [P, RING, 2 * D])
    pT = put("pT", [P, 2, P])
    put = region(RNG + 65536 + 1536, RNG + 65536 + 9728)
    xn2c = put("xn2c", [P, D])
    cand = put("cand", [P, TOPK, TOPK])
    crep = put("crep", [P, TOPK, TOPK])
    hot = put("hot", [P, 2, TOPK, TOPK])
    put = region(R2 + 4096 + 18688 + 64, END)
    x3 = put("x3", [P, D])
    xn3 = put("xn3", [P, D])
    xn3T = put("xn3T", [P, KD, P])
    srep = region(R2 + 4096 + 18688 + 64, END)("srep", [P, NT, NKEY])
    gfin = put("gfin", [P, D])
    dg = put("dg", [P, 4, P])

    psA = ctx.enter_context(nc.psum_tensor("psA", [P, 3, 512], F32))
    psB = ctx.enter_context(nc.psum_tensor("psB", [P, 3, 512], F32))
    psC = ctx.enter_context(nc.psum_tensor("psC", [P, 2, 512], F32))
    acc = psC[:, :, :].rearrange("p a n -> p (a n)")

    def alone(eng):
        eng.sem_inc(g.passed, 1)

    S = {}

    def sem(name):
        if name not in S:
            S[name] = ctx.enter_context(nc.semaphore(name))
        return S[name]

    def pieces(ps, buf, cols=CHUNKS):
        return [(ps[:, c, 0:n], buf[:, o:o + n]) for c, (o, n) in enumerate(cols)]

    names = """par_in s5s_in s5_in dbc_in wxa_in ident_ok ss_ok ms_ok sq_ok xn_ok xnT_tr xnT_ok s5_act s5_arg
      s5_ready m1_tr m1_ok k_mm k_ok m3_zero m3_in xa_mm xa_ok ust_ok scr_out us_in ut_tr ut_ok v_mm v_ok
      h0_in chain_ok y1_mm kd_ok y1_ok y1s_ok st_out w_xb_in w_gb_in w_ri_in xb_mm xb_ok gb_mm gb_ok
      conv_ok gate_mm gate_ok tanh_ok den_ok sqrt_ok yb_ok hcol_ok y2_mm y2_out y2_ok gelu_ok ya_tr ya_ok
      glu_mm sig_ok ya_done wglu_in s5_out w_ga_in w_ya_in w_gp_in w_yb_in ga_mm ya_mm gp_mm yb_mm sga_ok
      mga_ok sgb_ok mg_ok wout_in gffn_in o_mm x2_ok ss2_ok ms2_ok sq2_ok xn2_ok xn2_tr xn2T_ok keys_in
      w_q0_in w_q1_in q_mm qT_ok sc_mm top_ok wg_in wp_in pT_in idx_ok l2_top l2_exp dot_ok act_ok diag_ok
      slot_free acc_done x3_ok ss3_ok ms3_ok sq3_ok xn3_ok xn3_tr xn3T_ok gate3_mm gate3_ok ple_mm x4_ok
      ss4_ok ms4_ok sq4_ok y_ok y_out passed v_tail v_own a_own p_own v_g g_sv""".split()
    for n in names:
        sem(n)
    gathered = [sem(f"gathered{i}") for i in range(RING)]
    g = type("Sems", (), {n: S[n] for n in names})

    block = ctx.enter_context(nc.Block())

    @block.sync
    def _(sp):
        sp.dma_start(s5s[:, 0:3, :], a["s5_small"]).then_inc(g.s5s_in, 16)
        for i, (t0, t1) in enumerate(LOADS):
            n = rows_of(t0)
            sp.dma_start(xtok[0:n, t0:t1, :], a["x"][P * t0:P * (t1 - 1) + n, :].rearrange(
                "(t p) d -> p t d", p=n)).then_inc(sem(f"x_in{i}"), 16)
            if i == 0:
                sp.dma_start(par[:], a["par"]).then_inc(g.par_in, 16)
        sp.dma_start(s5w[:], a["s5_w"]).then_inc(g.s5_in, 16)
        sp.dma_start(dbc[:], a["s5_d"].partition_broadcast(P)).then_inc(g.dbc_in, 16)
        sp.dma_start(wxa[:], a["w_xa"]).then_inc(g.wxa_in, 16)
        sp.wait_ge(g.ust_ok, 1)
        sp.dma_start(a["scr"], ust[:]).then_inc(g.scr_out, 16)
        sp.wait_ge(g.scr_out, 16)
        sp.wait_ge(g.s5_ready, 2)
        sp.wait_ge(g.k_mm, 8)
        for grp in range(NG):
            sp.dma_start(u_s[:, grp], a["scr"].rearrange("(b j) (g c) -> b g j c", j=STEP, c=GC)[:, grp]).then_inc(g.us_in, 16)
        sp.wait_ge(g.kd_ok, 1)
        sp.wait_ge(g.m3_zero, 1)
        for j in range(STEP):
            sp.dma_start(M3[GC * j:GC * (j + 1), :, GC * j:], Ksb[:, :, 0:P - GC * j]).then_inc(g.m3_in, 16)
        sp.wait_ge(g.m1_tr, 8)
        sp.dma_start(V[:, NB + 1:NB + 1 + SB, :, :], a["h_s5"]).then_inc(g.h0_in, 16)
        sp.wait_ge(g.y1_mm, 16)
        sp.wait_ge(g.ust_ok, 1)
        def load(w, src, n, got):
            sp.dma_start(w, a[src][bass.ds(n, 1)].rearrange("a p k c -> p (a k) c")).then_inc(got, 16)
        load(w_xb[:], "w_xb", 0, g.w_xb_in)
        load(w_gb[:], "w_gb", 0, g.w_gb_in)
        load(w_ri[:], "w_ri", 0, g.w_ri_in)
        with sp.Fori(1, KD) as h:
            sp.wait_ge(g.xb_mm, h)
            load(w_xb[:], "w_xb", h, g.w_xb_in)
            sp.wait_ge(g.gb_mm, h)
            load(w_gb[:], "w_gb", h, g.w_gb_in)
            sp.wait_ge(g.gate_mm, h * 6)
            load(w_ri[:], "w_ri", h, g.w_ri_in)
        sp.wait_ge(g.chain_ok, 2)
        sp.dma_start(a["o_s5"][:, 0:1], V[:, NB:NB + 1, :, :]).then_inc(g.s5_out, 16)
        sp.dma_start(a["o_s5"][:, 1:1 + SB], V[:, NB + 1 + SB:SLOTS, :, :]).then_inc(g.s5_out, 16)
        sp.wait_ge(g.gelu_ok, 2)
        sp.dma_start(wglu[:], a["w_glu"]).then_inc(g.wglu_in, 16)
        slots = ((w_ga, "w_ga", g.w_ga_in, g.ga_mm), (w_ya, "w_ya", g.w_ya_in, g.ya_mm),
                 (w_gp, "w_gp", g.w_gp_in, g.gp_mm), (w_yb, "w_yb", g.w_yb_in, g.yb_mm))
        sp.wait_ge(g.gb_mm, KD)
        load(w_ga[:], "w_ga", 0, g.w_ga_in)
        load(w_gp[:], "w_gp", 0, g.w_gp_in)
        sp.wait_ge(g.gate_mm, 6 * KD)
        load(w_ya[:], "w_ya", 0, g.w_ya_in)
        sp.wait_ge(g.yb_ok, KD)
        load(w_yb[:], "w_yb", 0, g.w_yb_in)
        sp.dma_start(a["o_lru"], nlru[:]).then_inc(g.st_out, 16)
        sp.dma_start(a["o_conv"], nconv[:]).then_inc(g.st_out, 16)
        sp.wait_ge(g.glu_mm, 4)
        sp.wait_ge(g.ya_done, 1)
        sp.dma_start(wout[:], a["w_out"]).then_inc(g.wout_in, 16)
        with sp.Fori(1, KD) as m:
            for w, src, got, used in slots:
                sp.wait_ge(used, m)
                load(w[:], src, m, got)
        sp.wait_ge(g.mg_ok, KD + 1)
        sp.dma_start(gffn[:], a["g_ffn"].partition_broadcast(P)).then_inc(g.gffn_in, 16)
        load(w_q[:, 0], "w_q", 0, g.w_q0_in)
        load(w_q[:, 1], "w_q", 1, g.w_q1_in)
        for t in range(NT):
            if t >= 2:
                sp.wait_ge(g.x2_ok, t - 1)
            sp.dma_start(xr[0:rows_of(t), t % 2, :], a["x"][P * t:P * t + rows_of(t), :]).then_inc(sem(f"xr_in{t % 2}"), 16)
        sp.wait_ge(g.o_mm, NT)
        sp.dma_start(keys[:], a["keys"]).then_inc(g.keys_in, 16)
        sp.dma_start(wgate[:], a["w_gate"]).then_inc(g.wg_in, 16)
        sp.dma_start(wple[:], a["w_ple"]).then_inc(g.wp_in, 16)
        sp.wait_ge(g.xn2_tr, NT)
        sp.dma_start(gfin[:], a["g_final"].partition_broadcast(P)).then_inc(g.y_out, 16)
        with sp.Fori(1, HEADS) as h:
            for s, got in ((0, g.w_q0_in), (1, g.w_q1_in)):
                sp.wait_ge(g.q_mm, h * 6 + 3 * s - 3)
                load(w_q[:, s], "w_q", h * 2 + s, got)
        sp.wait_ge(g.sc_mm, 2 * HEADS)
        sp.dma_start(pT[:], a["p_T"][:, :, 0:P]).then_inc(g.pT_in, 16)

        def store(t, rows):
            sp.wait_ge(g.y_ok, t + 1)
            sp.dma_start(a["o_y"][bass.ds(t * P, rows), :], xn3[0:rows, :]).then_inc(g.y_out, 16)
        with sp.Fori(1, NT - 1) as t:
            sp.wait_ge(g.ple_mm, t)
            sp.dma_start(pT[:], a["p_T"][:, :, bass.ds(t * P, P)]).then_inc(g.pT_in, 16)
            store(t - 1, P)
        sp.wait_ge(g.ple_mm, NT - 1)
        sp.dma_start(pT[:, :, 0:TS], a["p_T"][:, :, TP:T]).then_inc(g.pT_in, 16)
        store(NT - 2, P)
        store(NT - 1, TS)
        sp.wait_ge(g.y_out, 16 * (NT + 1))
        sp.wait_ge(g.st_out, 32)
        sp.wait_ge(g.s5_out, 32)

    @block.gpsimd
    def _(pool):
        own = Chain(pool, g.p_own)
        own(nc.gpsimd.memset(ident[:], 0.0))
        nc.gpsimd.affine_select(out=ident[:], in_=ident[:], compare_op=ALU.not_equal, fill=1.0, base=0,
                                pattern=[[-1, P]], channel_multiplier=1).then_inc(g.ident_ok, 1)
        own(nc.gpsimd.iota(iota[:], pattern=[[1, TOPK]], base=0, channel_multiplier=0,
                           allow_small_or_imprecise_dtypes=True))
        nc.gpsimd.memset(M3[:], 0.0).then_inc(g.m3_zero, 1)
        pool.wait_ge(g.v_ok, PAIRS + 1)
        pool.wait_ge(g.h0_in, 16)

        with pool.Fori(0, NB) as c:
            own.enter(c * 3)
            prev = V[:, bass.ds(c, 1)].rearrange("p a i g -> p (a i) g")
            here = V[:, bass.ds(c + 1, 1)].rearrange("p a i g -> p (a i) g")
            own(nc.gpsimd.tensor_tensor(cp_t[:], A8[:], prev.unsqueeze(1).broadcast_to([P, 2, 2, PAIRS]), ALU.mult))
            own(nc.gpsimd.tensor_tensor(cp_u[:], cp_t[:, :, 0, :], cp_t[:, :, 1, :], ALU.add))
            own(nc.gpsimd.tensor_tensor(here, here, cp_u[:], ALU.add))
        own.leave(NB, 3)
        nc.gpsimd.tensor_copy(cp_u[:], cp_u[:]).then_inc(g.chain_ok, 1)
        ini = V[:, NB + 1:NB + 1 + SB]
        fin = V[:, NB + 1 + SB:SLOTS]
        for o in range(2):
            own(nc.gpsimd.tensor_tensor(cs_t[:], ini, A8[:, o:o + 1].broadcast_to([P, SB, 2, PAIRS]), ALU.mult))
            for i in range(2):
                own(nc.gpsimd.tensor_tensor(fin[:, :, o], fin[:, :, o], cs_t[:, :, i], ALU.add))
        nc.gpsimd.tensor_copy(cp_u[:], cp_u[:]).then_inc(g.chain_ok, 1)
        pool.wait_ge(g.y1_ok, 8)
        pool.wait_ge(g.y1s_ok, 8)
        for b in range(8):
            for w, (staged, buf) in enumerate(((y2st, u_c), (y2st_s, u_s))):
                pool.wait_ge(g.y2_out, 2 * b + w + 1)
                view = buf[:, groups(b)].rearrange("p q j c -> p q (j c)")
                nc.gpsimd.tensor_tensor(view, view, staged[:, b % 4, :].rearrange("p (q n) -> p q n", q=4),
                                        ALU.add).then_inc(g.y2_ok, 1)
        pool.wait_ge(g.x2_ok, NT)
        nc.gpsimd.memset(sv[:, UNITS - HEADS:UNITS + 1], 0.0).then_inc(g.g_sv, 1)
        nc.gpsimd.memset(si[:, UNITS - HEADS:UNITS + 1], 0.0).then_inc(g.g_sv, 1)

        def gather(u, s, rows):
            pool.wait_ge(g.idx_ok, u + 1)
            for k in range(TOPK):
                pool.wait_ge(g.slot_free, u * TOPK + (k + 1))
                alone(pool)
                pool.indirect_dma_start(
                    out=ring[0:rows, k % RING, :], out_offset=None, in_=a["uv"],
                    in_offset=bass.IndirectOffsetOnAxis(ap=idxu[0:rows, s, k:k + 1], axis=0),
                ).then_inc(gathered[k % RING], 16)
        with pool.Fori(0, (UNITS - HEADS) // 2) as w:
            for s in range(2):
                gather(w * 2 + s, s, P)
        with pool.Fori((UNITS - HEADS) // 2, UNITS // 2) as w:
            for s in range(2):
                gather(w * 2 + s, s, TS)

    @block.tensor
    def _(pe):
        def transposes(dst, srcs, done=None):
            for d, s in zip(dst, srcs):
                k = s.shape[0]
                b = s.start_partition if not callable(s.start_partition) else s.start_partition()
                ins = nc.tensor.transpose(d, s, ident[b:b + k, b:b + k])
            if done is not None:
                ins.then_inc(done, 1)

        def product(ps, w, cols, moving, done):
            n = w.shape[1]
            for c, (o, width) in enumerate(CHUNKS):
                for k in range(n):
                    ins = nc.tensor.matmul(ps[:, c, 0:width], w[:, k, cols], moving[:, k, o:o + width],
                                           start=(k == 0), stop=(k == n - 1))
            ins.then_inc(done, 1)

        pe.wait_ge(g.ident_ok, 1)
        for t in range(NT):
            n = rows_of(t)
            pe.wait_ge(g.xn_ok, t + 1)
            if t >= 2:
                pe.wait_ge(g.xnT_ok, t - 1)
            ps = (psA, psB)[t % 2]
            transposes([ps[:, k // 4, P * (k % 4):P * (k % 4) + n] for k in range(KD)],
                       [xtok[0:n, t, P * k:P * (k + 1)] for k in range(KD)], g.xnT_tr)
        pe.wait_ge(g.xnT_ok, NT)
        pe.wait_ge(g.wxa_in, 16)
        for k in range(KD):
            ins = nc.tensor.matmul(psC[0:TS, 1, :], xnT[:, k, TP:T], wxa[:, k, :], start=(k == 0), stop=(k == KD - 1))
        ins.then_inc(g.xa_mm, 1)

        def s5_inputs(steps):
            for j in steps:
                if j == 1:
                    pe.wait_ge(g.ust_ok, 1)
                if j >= 2:
                    pe.wait_ge(g.xa_ok, j - 1)
                for k in range(KD):
                    ins = nc.tensor.matmul(psC[:, j % 2, :], xnT[:, k, j:TP:STEP], wxa[:, k, :],
                                           start=(k == 0), stop=(k == KD - 1))
                ins.then_inc(g.xa_mm, 1)
        s5_inputs(range(0, XA_FIRST))
        pe.wait_ge(g.s5_ready, 1)
        for b in range(8):
            if b >= 2:
                pe.wait_ge(g.m1_ok, b - 1)
            for q in range(4):
                grp = group_of(b, q)
                lo = NS * (grp % 2)
                for ri in range(2):
                    ins = nc.tensor.transpose(
                        psA[:, b % 2, P * q + NS * ri:P * q + NS * (ri + 1)],
                        M1T[lo:lo + NS, grp // 2, ri].rearrange("p j c -> p (j c)"), ident[lo:lo + NS, lo:lo + NS])
            ins.then_inc(g.m1_tr, 1)
        pe.wait_ge(g.s5_ready, 2)
        for b in range(8):
            if b >= 2:
                pe.wait_ge(g.k_ok, b - 1)
            for q in range(4):
                grp = group_of(b, q)
                lo = NS * (grp % 2)
                for ri in range(2):
                    ins = nc.tensor.matmul(
                        psB[0:GC, b % 2, P * q:P * (q + 1)], bb[lo:lo + NS, ri, grp // 2, :],
                        CX[lo:lo + NS, grp // 2, ri, 0:STEP, :].rearrange("p n c -> p (n c)"),
                        start=(ri == 0), stop=(ri == 1))
            ins.then_inc(g.k_mm, 1)
        s5_inputs(range(XA_FIRST, STEP))
        pe.wait_ge(g.xa_ok, STEP)
        pe.wait_ge(g.m1_ok, 8)
        for b in range(8):
            if b >= 2:
                pe.wait_ge(g.ut_ok, b - 1)
            for q in range(4):
                grp = group_of(b, q)
                ins = nc.tensor.transpose(psA[:, b % 2, P * q:P * (q + 1)], u_c[:, grp].rearrange("p j c -> p (j c)"), ident[:])
            ins.then_inc(g.ut_tr, 1)
        pe.wait_ge(g.us_in, 16 * NG)
        for grp in range(NG):
            ins = nc.tensor.transpose(psA[:, 2, SB * grp:SB * (grp + 1)], u_s[:, grp].rearrange("p j c -> p (j c)"),
                                      ident[0:SB, 0:SB])
        ins.then_inc(g.ut_tr, 1)
        pe.wait_ge(g.ut_ok, 9)
        for q in range(PAIRS):
            if q >= 2:
                pe.wait_ge(g.v_ok, q - 1)
            for h in range(2):
                for ri in range(2):
                    ins = nc.tensor.matmul(psC[NS * h:NS * (h + 1), q % 2, 256 * ri:256 * ri + NB + SB],
                                           M1[:, 2 * q + h, NS * ri:NS * (ri + 1)], uT[:, 2 * q + h, :],
                                           start=True, stop=True, skip_group_check=True)
            ins.then_inc(g.v_mm, 1)
        pe.wait_ge(g.m3_in, 16 * STEP)
        for b in range(8):
            if b >= 2:
                pe.wait_ge(g.y1_ok, b - 1)
                pe.wait_ge(g.y1s_ok, b - 1)
            for q in range(4):
                grp = group_of(b, q)
                ins = nc.tensor.matmul(psA[:, b % 2, P * q:P * (q + 1)], uT[:, grp, 0:NB], M3[:, grp, :],
                                       start=True, stop=True)
            ins.then_inc(g.y1_mm, 1)
            for q in range(4):
                grp = group_of(b, q)
                ins = nc.tensor.matmul(psB[0:SB, b % 2, P * q:P * (q + 1)], uT[:, grp, NB:NB + SB], M3[:, grp, :],
                                       start=True, stop=True)
            ins.then_inc(g.y1_mm, 1)
        pe.wait_ge(g.y1_ok, 8)
        pe.wait_ge(g.y1s_ok, 8)
        def lru_inputs(h):
            pe.wait_ge(g.w_xb_in, h * 16 + 16)
            product(psA, w_xb, slice(0, P), xnT, g.xb_mm)
            pe.wait_ge(g.w_gb_in, h * 16 + 16)
            product(psB, w_gb, slice(0, P), xnT, g.gb_mm)

        def lru_gates(h):
            pe.wait_ge(g.conv_ok, h + 1)
            pe.wait_ge(g.w_ri_in, h * 16 + 16)
            for c, (o, n) in enumerate(CHUNKS):
                for r in range(2):
                    if c > 0:
                        pe.wait_ge(g.gate_ok, h * 6 + (2 * c + r - 1))
                    nc.tensor.matmul(psC[:, r, 0:n], w_ri[:, r, :], xc[:, o:o + n], start=True,
                                     stop=True).then_inc(g.gate_mm, 1)
            pe.wait_ge(g.xb_ok, h + 1)
            pe.wait_ge(g.gb_ok, h + 1)
        with pe.Fori(0, KD - 1) as h:
            lru_inputs(h)
            lru_gates(h)
        pe.wait_ge(g.chain_ok, 2)
        for b in range(8):
            if b >= 2:
                pe.wait_ge(g.y2_out, 2 * b - 2)
            for ps, n, s0 in ((psA, NB, 0), (psB, SB, NB + 1)):
                for q in range(4):
                    grp = group_of(b, q)
                    lo = NS * (grp % 2)
                    for ri in range(2):
                        ins = nc.tensor.matmul(
                            ps[0:n, b % 2, P * q:P * (q + 1)], V[lo:lo + NS, s0:s0 + n, ri, grp // 2],
                            CX[lo:lo + NS, grp // 2, ri, 1:STEP + 1, :].rearrange("p n c -> p (n c)"),
                            start=(ri == 0), stop=(ri == 1))
                ins.then_inc(g.y2_mm, 1)
        pe.wait_ge(g.y2_out, 16)
        lru_inputs(KD - 1)
        pe.wait_ge(g.gelu_ok, 2)
        pe.wait_ge(g.gate_ok, 6 * (KD - 1))
        for j in range(STEP):
            if j >= 2:
                pe.wait_ge(g.ya_ok, j - 1)
            transposes([psC[:, j % 2, P * f:P * (f + 1)] for f in range(4)],
                       [y_c[:, j, P * f:P * (f + 1)] for f in range(4)], g.ya_tr)
        pe.wait_ge(g.xb_ok, KD)
        for j in range(STEP):
            for f in range(4):
                o = (f * STEP + j) * SB
                ins = nc.tensor.transpose(psA[:, 2, o:o + SB], y_s[:, j, P * f:P * (f + 1)], ident[0:SB, 0:SB])
        ins.then_inc(g.ya_tr, 1)
        pe.wait_ge(g.ya_ok, STEP)
        lru_gates(KD - 1)
        pe.wait_ge(g.ya_ok, STEP + 1)
        pe.wait_ge(g.wglu_in, 16)
        for m in range(4):
            ps = (psA, psB)[m % 2]
            if m >= 2:
                pe.wait_ge(g.sig_ok, m - 1)
            product(ps, wglu, slice(P * m, P * (m + 1)), yaT, g.glu_mm)
        pe.wait_ge(g.sig_ok, 3)
        with pe.Fori(0, KD) as m:
            pe.wait_ge(g.w_ga_in, m * 16 + 16)
            product(psA, w_ga, slice(0, P), xnT, g.ga_mm)
            pe.wait_ge(g.mg_ok, m + 1)
            pe.wait_ge(g.w_ya_in, m * 16 + 16)
            pe.wait_ge(g.ya_done, 1)
            product(psB, w_ya, slice(0, P), yaT, g.ya_mm)
            pe.wait_ge(g.sga_ok, m + 1)
            pe.wait_ge(g.w_gp_in, m * 16 + 16)
            product(psA, w_gp, slice(0, P), xnT, g.gp_mm)
            pe.wait_ge(g.mga_ok, m + 1)
            pe.wait_ge(g.w_yb_in, m * 16 + 16)
            pe.wait_ge(g.yb_ok, KD)
            product(psB, w_yb, slice(0, P), ybT, g.yb_mm)
            pe.wait_ge(g.sgb_ok, m + 1)
        pe.wait_ge(g.mg_ok, KD + 1)
        pe.wait_ge(g.wout_in, 16)

        def x2_transposes(t):
            n = rows_of(t)
            ps = psA if t < NT - 1 else psB
            pe.wait_ge(g.xn2_ok, t + 1)
            if t >= 1:
                pe.wait_ge(g.xn2T_ok, t)
            transposes([ps[:, k // 4, P * (k % 4):P * (k % 4) + n] for k in range(KD)],
                       [xn2s[0:n, t % 2, P * k:P * (k + 1)] for k in range(KD)], g.xn2_tr)
        for t in range(NT):
            n = rows_of(t)
            ps = (psC, psB)[t % 2]
            if t >= 2:
                pe.wait_ge(g.x2_ok, t - 1)
            for half in range(2):
                for k in range(KD):
                    ins = nc.tensor.matmul(ps[0:n, half, :], mgT[:, k, P * t:P * t + n],
                                           wout[:, k, 512 * half:512 * (half + 1)], start=(k == 0), stop=(k == KD - 1))
            ins.then_inc(g.o_mm, 1)
            if t >= 1:
                x2_transposes(t - 1)

        def query(s, chunks):
            for c in chunks:
                o, n = CHUNKS[c]
                for k in range(KD):
                    ins = nc.tensor.matmul(psA[:, c, 0:n], w_q[:, s, k, :], xn2T[:, k, o:o + n],
                                           start=(k == 0), stop=(k == KD - 1))
                ins.then_inc(g.q_mm, 1)

        def next_query(h, j):
            s = j % 2
            pe.wait_ge((g.w_q0_in, g.w_q1_in)[s], h * 16 + 16 * (1 + j // 2))
            for c in range(3):
                pe.wait_ge(g.qT_ok, h * 6 + (3 * j + c - 2))
                query(s, [c])

        def scores(h, s, ps=psB):
            pe.wait_ge(g.qT_ok, h * 6 + (3 * s + 3))
            if ps is psB:
                pe.wait_ge(g.top_ok, h * 2 + (s + 1))
            for t in range(NT):
                n = rows_of(t)
                ins = nc.tensor.matmul(ps[0:n, t // 4, P * (t % 4):P * (t % 4 + 1)], qT[:, s, P * t:P * t + n],
                                       keys[:, bass.ds(h * 2 + s, 1), :].rearrange("p a n -> p (a n)"),
                                       start=True, stop=True)
            ins.then_inc(g.sc_mm, 1)
        pe.wait_ge(g.w_q0_in, 16)
        pe.wait_ge(g.xn2T_ok, NT - 1)
        query(0, [0, 1])
        x2_transposes(NT - 1)
        pe.wait_ge(g.xn2T_ok, NT)
        query(0, [2])
        pe.wait_ge(g.keys_in, 16)
        with pe.Fori(0, HEADS - 1) as h:
            next_query(h, 1)
            scores(h, 0)
            next_query(h, 2)
            scores(h, 1)
        next_query(HEADS - 1, 1)
        over_keys = RING - (VREG - RNG) // (8 * D)
        nc.tensor.transpose(psC[:, 0, 0:P], ident[:], ident[:]).then_inc(g.slot_free, RING - over_keys)
        scores(HEADS - 1, 0)
        scores(HEADS - 1, 1, psA)
        nc.tensor.transpose(psC[:, 0, 0:P], ident[:], ident[:]).then_inc(g.slot_free, over_keys)

        def experts(u, rows, last=False, between={}):
            for k in range(TOPK):
                pe.wait_ge(g.diag_ok, u * TOPK + (k + 1))
                alone(pe)
                for half in range(2):
                    ins = nc.tensor.matmul(acc[0:rows, 512 * half:512 * (half + 1)], dg[0:rows, k % 4, 0:rows],
                                           ring[0:rows, k % RING, D + 512 * half:D + 512 * (half + 1)],
                                           start=False, stop=(last and k == TOPK - 1))
                ins.then_inc(g.slot_free, 1)
                for step in between.get(k, ()):
                    step()

        def embedding(t, rows):
            def turn():
                pe.wait_ge(g.xn3_ok, t + 1)
                alone(pe)
                transposes([psA[:, k // 4, P * (k % 4):P * (k % 4) + rows] for k in range(KD)],
                           [xn3[0:rows, P * k:P * (k + 1)] for k in range(KD)], g.xn3_tr)

            def step(ps, x, w, n, half, k, first, done):
                def run():
                    if first:
                        pe.wait_ge(g.pT_in, t * 16 + 16)
                        pe.wait_ge(g.xn3T_ok, t + 1)
                        alone(pe)
                    ins = nc.tensor.matmul(ps[0:rows, half, :], x[:, k, 0:rows], w[:, k, 512 * half:512 * (half + 1)],
                                           start=(k == 0), stop=(k == n - 1))
                    if half == 1 and k == n - 1:
                        ins.then_inc(done, 1)
                return run
            todo = [step(psA, pT, wple, 2, half, k, half + k == 0, g.ple_mm) for half in range(2) for k in range(2)]
            todo += [step(psB, xn3T, wgate, KD, half, k, False, g.gate3_mm) for half in range(2) for k in range(KD)]
            return turn, todo

        def tile(t, rows, before):
            if before:
                pe.wait_ge(g.x3_ok, t)
                alone(pe)
            for half in range(2):
                nc.tensor.matmul(acc[0:rows, 512 * half:512 * (half + 1)], ident[0:rows, 0:rows],
                                 x2[0:rows, bass.ds(t, 1), 512 * half:512 * (half + 1)].rearrange("p a n -> p (a n)"),
                                 start=True, stop=False)
            first, second = {}, {}
            if before:
                turn, todo = embedding(t - 1, P)
                first[6] = [turn]
                for k in range(9, TOPK):
                    first[k] = [todo.pop(0), todo.pop(0)]
                for k in range(3):
                    second[k] = [todo.pop(0), todo.pop(0)]
                assert not todo
            experts(t * HEADS, rows, between=first)
            experts(t * HEADS + 1, rows, between=second)
            with pe.Fori(1, HEADS // 2 - 1) as w:
                for s in range(2):
                    experts(t * HEADS + w * 2 + s, rows)
            experts(t * HEADS + 6, rows)
            experts(t * HEADS + 7, rows, last=True)
            nc.tensor.transpose(psB[0:rows, 2, 0:rows], ident[0:rows, 0:rows], ident[0:rows, 0:rows]).then_inc(g.acc_done, 1)

        pe.wait_ge(g.wg_in, 16)
        pe.wait_ge(g.wp_in, 16)
        tile(0, P, False)
        with pe.Fori(1, NT - 1) as t:
            tile(t, P, True)
        tile(NT - 1, TS, True)
        turn, todo = embedding(NT - 1, TS)
        for step in [turn] + todo:
            step()

    @block.scalar
    def _(sc):
        own = Chain(sc, g.a_own)
        for i, (t0, t1) in enumerate(LOADS):
            n = rows_of(t0)
            sc.wait_ge(sem(f"x_in{i}"), 16)
            for t in range(t0, t1):
                own(nc.scalar.activation(acc[0:n, :], xtok[0:n, t, :], ACT.Square, accum_out=sumsq[0:n, t:t + 1]))
            nc.scalar.activation(sumsq[0:n, t0:t1], sumsq[0:n, t0:t1], ACT.Copy).then_inc(g.ss_ok, 1)
            sc.wait_ge(g.ms_ok, i + 1)
            nc.scalar.activation(rstd[0:n, t0:t1], rstd[0:n, t0:t1], ACT.Sqrt).then_inc(g.sq_ok, 1)
        sc.wait_ge(g.s5_arg, 1)
        nc.scalar.activation(s5s[:, 8:10, :], s5s[:, 6:8, :], ACT.Sin).then_inc(g.s5_act, 1)
        sc.wait_ge(g.xa_mm, 1)
        nc.scalar.activation(ust[:], psC[0:TS, 1, :], ACT.Copy).then_inc(g.ust_ok, 1)

        def s5_inputs(steps):
            for j in steps:
                sc.wait_ge(g.xa_mm, j + 2)
                nc.scalar.activation(u_c[:, :, j, :], psC[:, j % 2, :].rearrange("p (g c) -> p g c", g=NG),
                                     ACT.Copy).then_inc(g.xa_ok, 1)
        s5_inputs(range(0, XA_FIRST))
        sc.wait_ge(g.xnT_ok, NT)
        for b in range(8):
            sc.wait_ge(g.m1_tr, b + 1)
            nc.scalar.activation(M1[:, groups(b), :], psA[:, b % 2, :].rearrange("p (q n) -> p q n", q=4),
                                 ACT.Copy).then_inc(g.m1_ok, 1)
        for b in range(8):
            sc.wait_ge(g.k_mm, b + 1)
            nc.scalar.activation(Ksb[:, groups(b), :], psB[0:GC, b % 2, :].rearrange("p (q n) -> p q n", q=4),
                                 ACT.Copy).then_inc(g.k_ok, 1)
        s5_inputs(range(XA_FIRST, STEP))
        for b in range(8):
            sc.wait_ge(g.ut_tr, b + 1)
            nc.scalar.activation(uT[:, groups(b), 0:NB], psA[:, b % 2, :].rearrange("p (q n) -> p q n", q=4),
                                 ACT.Copy).then_inc(g.ut_ok, 1)
        sc.wait_ge(g.ut_tr, 9)
        nc.scalar.activation(uT[:, :, NB:NB + SB], psA[:, 2, 0:NG * SB].rearrange("p (q n) -> p q n", q=NG),
                             ACT.Copy).then_inc(g.ut_ok, 1)
        for b in range(8):
            sc.wait_ge(g.y1_mm, 2 * b + 1)
            nc.scalar.activation(u_c[:, groups(b)].rearrange("p q j c -> p q (j c)"),
                                 psA[:, b % 2, :].rearrange("p (q n) -> p q n", q=4), ACT.Copy).then_inc(g.y1_ok, 1)
        def lru_inputs(h):
            sc.wait_ge(g.xb_mm, h + 1)
            nc.scalar.activation(xpad[:, 3:387], psA[:, 0, 0:384], ACT.Copy)
            nc.scalar.activation(xpad[:, 387:771], psA[:, 1, 0:384], ACT.Copy)
            nc.scalar.activation(xpad[:, 771:1027], psA[:, 2, 0:256], ACT.Copy)
            nc.scalar.activation(xpads[:, :, 3:11], psA[:, 2, 256:320].rearrange("p (b l) -> p b l", b=SB),
                                 ACT.Copy).then_inc(g.xb_ok, 1)
            sc.wait_ge(g.gb_mm, h + 1)
            for c, (src, dst) in enumerate(pieces(psB, gg)):
                ins = nc.scalar.activation(dst, src, ACT.Gelu_apprx_tanh)
            ins.then_inc(g.gb_ok, 1)

        def lru_gates(h):
            sc.wait_ge(g.hcol_ok, h + 1)
            for c, (o, n) in enumerate(CHUNKS):
                for r, buf in ((0, rt), (1, ig)):
                    sc.wait_ge(g.gate_mm, h * 6 + (2 * c + r + 1))
                    nc.scalar.activation(buf[:, o:o + n], psC[:, r, 0:n], ACT.Sigmoid,
                                         bias=hpar[:, 5 + r:6 + r]).then_inc(g.gate_ok, 1)

        def lru_roots(h):
            sc.wait_ge(g.gate_ok, h * 6 + 6)
            nc.scalar.activation(rt[:], rt[:], ACT.Tanh, scale=hpar[:, 7:8]).then_inc(g.tanh_ok, 1)
            sc.wait_ge(g.den_ok, h + 1)
            nc.scalar.activation(rt[:], rt[:], ACT.Sqrt, scale=-4.0).then_inc(g.sqrt_ok, 1)
        with sc.Fori(0, KD - 2) as h:
            lru_inputs(h)
            lru_gates(h)
            lru_roots(h)
            sc.wait_ge(g.yb_ok, h + 1)
        lru_inputs(KD - 2)
        lru_gates(KD - 2)
        for b in range(8):
            for w, (ps, staged, n) in enumerate(((psA, y2st, NB), (psB, y2st_s, SB))):
                sc.wait_ge(g.y2_mm, 2 * b + w + 1)
                if b >= 4:
                    sc.wait_ge(g.y2_ok, 2 * (b - 4) + w + 1)
                nc.scalar.activation(staged[:, b % 4, :], ps[0:n, b % 2, :], ACT.Copy).then_inc(g.y2_out, 1)
        lru_roots(KD - 2)
        sc.wait_ge(g.yb_ok, KD - 1)
        sc.wait_ge(g.y2_ok, 16)
        sc.wait_ge(g.s5_out, 32)
        nc.scalar.activation(y_c[:].rearrange("p j (g c) -> p g j c", g=NG), u_c[:], ACT.Gelu_apprx_tanh).then_inc(g.gelu_ok, 1)
        nc.scalar.activation(y_s[:].rearrange("p j (g c) -> p g j c", g=NG), u_s[:], ACT.Gelu_apprx_tanh).then_inc(g.gelu_ok, 1)
        lru_inputs(KD - 1)
        for j in range(STEP):
            sc.wait_ge(g.ya_tr, j + 1)
            nc.scalar.activation(yaT[:, :, j:TP:STEP], psC[:, j % 2, :].rearrange("p (f n) -> p f n", f=4),
                                 ACT.Copy).then_inc(g.ya_ok, 1)
        sc.wait_ge(g.ya_tr, STEP + 1)
        for f in range(4):
            ins = nc.scalar.activation(
                yaT[:, f, TP:T].rearrange("p (b j) -> p j b", b=SB),
                psA[:, 2, f * TS:(f + 1) * TS].rearrange("p (j b) -> p j b", j=STEP), ACT.Copy)
        ins.then_inc(g.ya_ok, 1)
        lru_gates(KD - 1)
        lru_roots(KD - 1)
        for m in range(4):
            sc.wait_ge(g.glu_mm, m + 1)
            ps = (psA, psB)[m % 2]
            for src, dst in pieces(ps, sig[:, m, :]):
                ins = nc.scalar.activation(dst, src, ACT.Sigmoid, bias=bglu[:, m:m + 1])
            ins.then_inc(g.sig_ok, 1)
        with sc.Fori(0, KD) as m:
            sc.wait_ge(g.ga_mm, m + 1)
            sc.wait_ge(g.mg_ok, m + 1)
            for src, dst in pieces(psA, sga):
                ins = nc.scalar.activation(dst, src, ACT.Sigmoid)
            ins.then_inc(g.sga_ok, 1)
            sc.wait_ge(g.gp_mm, m + 1)
            for src, dst in pieces(psA, sgb):
                ins = nc.scalar.activation(dst, src, ACT.Sigmoid)
            ins.then_inc(g.sgb_ok, 1)
        for t in range(NT + 1):
            if t < NT:
                n = rows_of(t)
                sc.wait_ge(g.x2_ok, t + 1)
                if t >= 2:
                    sc.wait_ge(g.xn2_tr, t - 1)
                own(nc.scalar.activation(xn2s[0:n, t % 2, :], x2[0:n, t, :], ACT.Square,
                                         accum_out=sumsq2[0:n, t:t + 1]))
                nc.scalar.activation(sumsq2[0:n, t:t + 1], sumsq2[0:n, t:t + 1], ACT.Copy).then_inc(g.ss2_ok, 1)
                sc.wait_ge(g.ms2_ok, t + 1)
                nc.scalar.activation(rstd2[0:n, t:t + 1], rstd2[0:n, t:t + 1], ACT.Sqrt).then_inc(g.sq2_ok, 1)
            if t >= 1:
                n = rows_of(t - 1)
                sc.wait_ge(g.xn2_tr, t)
                ps = psA if t < NT else psB
                for b in range(2):
                    ins = nc.scalar.activation(xn2T[:, 4 * b:4 * b + 4, P * (t - 1):P * (t - 1) + n],
                                               ps[:, b, :].rearrange("p (k n) -> p k n", k=4)[:, :, 0:n], ACT.Copy)
                ins.then_inc(g.xn2T_ok, 1)
        with sc.Fori(0, HEADS) as h:
            for s in range(2):
                for c, (src, dst) in enumerate(pieces(psA, qT[:, s, :])):
                    sc.wait_ge(g.q_mm, h * 6 + (3 * s + c + 1))
                    nc.scalar.activation(dst, src, ACT.Copy).then_inc(g.qT_ok, 1)

        def softmax_exp(u):
            sc.wait_ge(g.l2_top, u + 1)
            nc.scalar.activation(expt[:], top[:], ACT.Exp, bias=gate_sum[:, 0:1],
                                 accum_out=gate_sum[:, 1:2])
            nc.scalar.activation(gate_sum[:, 3:4], gate_sum[:, 0:1], ACT.Copy).then_inc(g.l2_exp, 1)

        def activations(u, rows, between={}):
            for q in range(TOPK // 2):
                sc.wait_ge(g.dot_ok, u * 8 + (q + 1))
                nc.scalar.activation(act[0:rows, 2 * q:2 * q + 2], dot[0:rows, 2 * q:2 * q + 2],
                                     ACT.Gelu_apprx_tanh).then_inc(g.act_ok, 1)
                if q == 1:
                    softmax_exp(u + 1)
                for step in between.get(q, ()):
                    step()

        def embedding(t, rows):
            def out():
                sc.wait_ge(g.acc_done, t + 1)
                nc.scalar.activation(x3[0:rows, :], acc[0:rows, :], ACT.Copy).then_inc(g.x3_ok, 1)

            def squares(ready):
                def run():
                    if ready is None:
                        sc.wait_ge(g.x3_ok, t + 1)
                        sc.wait_ge(g.y_out, t * 16 + 16)
                    else:
                        sc.wait_ge(ready, t + 1)
                    nc.scalar.activation(xn3[0:rows, :], x3[0:rows, :], ACT.Square, accum_out=tail_s[0:rows, 0:1])
                    nc.scalar.activation(tail_s[0:rows, 3:4], x3[0:rows, 0:1], ACT.Copy).then_inc(
                        g.ss3_ok if ready is None else g.ss4_ok, 1)
                return run

            def root(ready, done):
                def run():
                    sc.wait_ge(ready, t + 1)
                    nc.scalar.activation(tail_s[0:rows, 1:2], tail_s[0:rows, 1:2], ACT.Sqrt).then_inc(done, 1)
                return run

            def gate():
                sc.wait_ge(g.gate3_mm, t + 1)
                nc.scalar.activation(xn3[0:rows, :], psB[0:rows, 0:2, :].rearrange("p a n -> p (a n)"),
                                     ACT.Sigmoid).then_inc(g.gate3_ok, 1)
            return (out, squares(None), root(g.ms3_ok, g.sq3_ok), gate, squares(g.x4_ok), root(g.ms4_ok, g.sq4_ok))

        def tile(t, rows, before):
            first, second = {}, {}
            if before:
                out, sq3, root3, gate, sq4, root4 = embedding(t - 1, P)
                out()
                first = {0: [sq3], 1: [root3]}
                second = {3: [gate], 4: [sq4], 6: [root4]}
            activations(t * HEADS, rows, first)
            activations(t * HEADS + 1, rows, second)
            with sc.Fori(2, HEADS) as h:
                activations(t * HEADS + h, rows)

        softmax_exp(0)
        tile(0, P, False)
        with sc.Fori(1, NT - 1) as t:
            tile(t, P, True)
        tile(NT - 1, TS, True)
        for step in embedding(NT - 1, TS):
            step()

    @block.vector
    def _(ve):
        own = Chain(ve, g.v_own)
        v = nc.vector

        def mean_root(dst, src, eps=EPS):
            own(v.tensor_scalar(dst, src, 1.0 / D, eps, ALU.mult, ALU.add))

        def exp_small(out, x, w):
            n, r, p = exs[:, 0, 0:w], exs[:, 1, 0:w], exs[:, 2, 0:w]
            own(v.tensor_scalar(n, x, 1.0 / math.log(2.0), MAGIC, ALU.mult, ALU.add))
            own(v.tensor_scalar(n, n, MAGIC, -126.0, ALU.subtract, ALU.max))
            own(v.tensor_scalar(n, n, 127.0, None, ALU.min))
            own(v.scalar_tensor_tensor(r, n, -0.693359375, x, ALU.mult, ALU.add))
            own(v.scalar_tensor_tensor(r, n, 2.12194440e-4, r, ALU.mult, ALU.add))
            own(v.tensor_scalar(p, r, 1.0 / 5040.0, None, ALU.mult))
            for c in (720.0, 120.0, 24.0, 6.0, 2.0, 1.0):
                own(v.scalar_tensor_tensor(p, p, 1.0 / c, r, ALU.add, ALU.mult))
            own(v.tensor_scalar(exi[:, 0:w], n, 127.0, 8388608.0, ALU.add, ALU.mult))
            own(v.scalar_tensor_tensor(out, p, 1.0, exi[:, 0:w].bitcast(F32), ALU.add, ALU.mult))

        def tt(out, x, y, op):
            own(v.tensor_tensor(out, x, y, op))

        q = s5s
        lr, li, ldt = q[:, 0], q[:, 1], q[:, 2]
        dt, mag, th = q[:, 3], q[:, 4], q[:, 5]
        rs, rc, sn, cs = q[:, 6], q[:, 7], q[:, 8], q[:, 9]
        t1, t2, t3 = q[:, 10], q[:, 11], q[:, 12]
        nr, den, cr, ci = q[:, 13], q[:, 14], q[:, 15], q[:, 16]
        ve.wait_ge(g.s5s_in, 16)
        exp_small(dt, ldt, PAIRS)
        tt(t1, lr, dt, ALU.mult)
        exp_small(mag, t1, PAIRS)
        tt(th, li, dt, ALU.mult)
        C1, C2 = 6.28125, 0.00193500518798828125
        C3 = 2 * math.pi - C1 - C2
        for dst, quarter in ((rs, 0.0), (rc, 0.25)):
            own(v.tensor_scalar(t1, th, 1.0 / (2 * math.pi), quarter, ALU.mult, ALU.add))
            own(v.tensor_scalar(t1, t1, MAGIC, None, ALU.add))
            own(v.tensor_scalar(t1, t1, MAGIC, None, ALU.subtract))
            own(v.scalar_tensor_tensor(dst, t1, -C1, th, ALU.mult, ALU.add))
            own(v.scalar_tensor_tensor(dst, t1, -C2, dst, ALU.mult, ALU.add))
            own(v.scalar_tensor_tensor(dst, t1, -C3, dst, ALU.mult, ALU.add))
            own(v.tensor_scalar(dst, dst, quarter * 2 * math.pi, 3.1415925, ALU.add, ALU.min))
            own(v.tensor_scalar(dst, dst, -3.1415925, None, ALU.max))
        own(v.tensor_copy(t1, t1))
        v.tensor_copy(t2, t1).then_inc(g.s5_arg, 1)
        def gains(t0, t1):
            for t in range(t0, t1):
                n = rows_of(t)
                ve.wait_ge(g.xnT_tr, t + 1)
                ps = (psA, psB)[t % 2]
                for b in range(2):
                    ins = v.tensor_tensor(xnT[:, 4 * b:4 * b + 4, P * t:P * t + n],
                                          ps[:, b, :].rearrange("p (k n) -> p k n", k=4)[:, :, 0:n],
                                          gmix[:, 4 * b:4 * b + 4].unsqueeze(2).broadcast_to([P, 4, n]), ALU.mult)
                ins.then_inc(g.xnT_ok, 1)
        for i, (lo, hi) in enumerate(LOADS):
            n = rows_of(lo)
            ve.wait_ge(g.ss_ok, i + 1)
            v.tensor_scalar(rstd[0:n, lo:hi], sumsq[0:n, lo:hi], 1.0 / D, EPS, ALU.mult, ALU.add).then_inc(g.ms_ok, 1)
            ve.wait_ge(g.sq_ok, i + 1)
            own(v.reciprocal(rstd[0:n, lo:hi], rstd[0:n, lo:hi]))
            for t in range(lo, hi):
                v.tensor_scalar(xtok[0:n, t, :], xtok[0:n, t, :], rstd[0:n, t:t + 1], None,
                                ALU.mult).then_inc(g.xn_ok, 1)
            if i == 1:
                ve.wait_ge(g.par_in, 16)
            if i >= 1:
                gains(*LOADS[i - 1])
        gains(*LOADS[-1])
        e, z, z2, pp = exs[:, 3, 0:8], exs[:, 4, 0:8], exs[:, 3, 8:16], exs[:, 4, 8:16]
        own(v.scalar_tensor_tensor(e, lam, -1.0, lam, ALU.mult, ALU.min))
        exp_small(z, e, 8)
        own(v.tensor_copy(e, z))
        own(v.tensor_scalar(z, e, 2.0, None, ALU.add))
        own(v.reciprocal(z, z))
        tt(z, z, e, ALU.mult)
        tt(z2, z, z, ALU.mult)
        own(v.tensor_scalar(pp, z2, 1.0 / 15.0, None, ALU.mult))
        for c in (13.0, 11.0, 9.0, 7.0, 5.0, 3.0):
            own(v.scalar_tensor_tensor(pp, pp, 1.0 / c, z2, ALU.add, ALU.mult))
        own(v.scalar_tensor_tensor(z, pp, 1.0, z, ALU.add, ALU.mult))
        own(v.tensor_scalar(e, lam, -1.0, 0.0, ALU.mult, ALU.max))
        own(v.scalar_tensor_tensor(z, z, 2.0, e, ALU.mult, ALU.add))
        own(v.tensor_scalar(spk[:], z, -4.0, None, ALU.mult))
        ve.wait_ge(g.s5_act, 1)
        own(v.memset(pw[:, 0, :, 0], 1.0))
        own(v.memset(pw[:, 1, :, 0], 0.0))
        tt(pw[:, 0, :, 1], mag, cs, ALU.mult)
        tt(pw[:, 1, :, 1], mag, sn, ALU.mult)
        ar, ai = pw[:, 0, :, 1], pw[:, 1, :, 1]
        for n in range(2, STEP + 1):
            pr, pi = pw[:, 0, :, n - 1], pw[:, 1, :, n - 1]
            tt(t1, pr, ar, ALU.mult)
            tt(t2, pi, ai, ALU.mult)
            tt(pw[:, 0, :, n], t1, t2, ALU.subtract)
            tt(t1, pr, ai, ALU.mult)
            tt(t2, pi, ar, ALU.mult)
            tt(pw[:, 1, :, n], t1, t2, ALU.add)
        own(v.tensor_copy(pwr[:], pw[:, :, :, STEP - 1::-1]))
        own(v.tensor_copy(A8[:, 0, 0], pw[:, 0, :, STEP]))
        own(v.tensor_scalar(A8[:, 0, 1], pw[:, 1, :, STEP], -1.0, None, ALU.mult))
        own(v.tensor_copy(A8[:, 1, 0], pw[:, 1, :, STEP]))
        own(v.tensor_copy(A8[:, 1, 1], pw[:, 0, :, STEP]))
        own(v.tensor_scalar(nr, ar, -1.0, None, ALU.add))
        tt(t1, lr, lr, ALU.mult)
        tt(t2, li, li, ALU.mult)
        tt(den, t1, t2, ALU.add)
        own(v.reciprocal(den, den))
        tt(t1, nr, lr, ALU.mult)
        tt(t2, ai, li, ALU.mult)
        tt(t1, t1, t2, ALU.add)
        tt(cr, t1, den, ALU.mult)
        tt(t1, ai, lr, ALU.mult)
        tt(t2, nr, li, ALU.mult)
        tt(t1, t1, t2, ALU.subtract)
        tt(ci, t1, den, ALU.mult)
        ve.wait_ge(g.s5_in, 16)
        crb, cib = (x.unsqueeze(2).broadcast_to([P, PAIRS, GC]) for x in (cr, ci))
        tb = tmpb[:, 0:PAIRS * GC].rearrange("p (g c) -> p g c", g=PAIRS)
        tt(bb[:, 0], s5w[:, 0], crb, ALU.mult)
        tt(tb, s5w[:, 1], cib, ALU.mult)
        tt(bb[:, 0], bb[:, 0], tb, ALU.subtract)
        tt(bb[:, 1], s5w[:, 1], crb, ALU.mult)
        tt(tb, s5w[:, 0], cib, ALU.mult)
        tt(bb[:, 1], bb[:, 1], tb, ALU.add)

        def spread(out, x, y, n, op):
            tt(out, x.unsqueeze(3).broadcast_to([P, PAIRS, n, GC]), y.unsqueeze(2).broadcast_to([P, PAIRS, n, GC]), op)
        tm = tmpb[:, 0:PAIRS * STEP * GC].rearrange("p (g n c) -> p g n c", g=PAIRS, n=STEP)
        spread(M1T[:, :, 0], pwr[:, 0], bb[:, 0], STEP, ALU.mult)
        spread(tm, pwr[:, 1], bb[:, 1], STEP, ALU.mult)
        tt(M1T[:, :, 0], M1T[:, :, 0], tm, ALU.subtract)
        spread(M1T[:, :, 1], pwr[:, 0], bb[:, 1], STEP, ALU.mult)
        spread(tm, pwr[:, 1], bb[:, 0], STEP, ALU.mult)
        v.tensor_tensor(M1T[:, :, 1], M1T[:, :, 1], tm, ALU.add).then_inc(g.s5_ready, 1)
        ve.wait_ge(g.s5_ready, 1)
        tm = tmpb[:, :].rearrange("p (g n c) -> p g n c", g=PAIRS, n=STEP + 1)
        spread(CX[:, :, 0], pw[:, 0], s5w[:, 2], STEP + 1, ALU.mult)
        spread(tm, pw[:, 1], s5w[:, 3], STEP + 1, ALU.mult)
        tt(CX[:, :, 0], CX[:, :, 0], tm, ALU.subtract)
        spread(CX[:, :, 1], pw[:, 0], s5w[:, 3], STEP + 1, ALU.mult)
        spread(tm, pw[:, 1], s5w[:, 2], STEP + 1, ALU.mult)
        for n in range(0, STEP + 1, 3):
            own(v.scalar_tensor_tensor(CX[:, :, 1, n:n + 3].rearrange("p g n c -> p g (n c)"),
                                       CX[:, :, 1, n:n + 3].rearrange("p g n c -> p g (n c)"), -1.0,
                                       tm[:, :, n:n + 3].rearrange("p g n c -> p g (n c)"), ALU.mult, ALU.subtract))
        v.tensor_copy(t2, t1).then_inc(g.s5_ready, 1)
        ve.wait_ge(g.dbc_in, 16)
        own(v.tensor_tensor(dk[:], dbc[0:GC].rearrange("p (g c) -> p g c", g=NG),
                            ident[0:GC, 0:GC].unsqueeze(1).broadcast_to([GC, NG, GC]), ALU.mult))
        ve.wait_ge(g.k_ok, 8)
        v.tensor_tensor(Ksb[:, :, 0:GC], Ksb[:, :, 0:GC], dk[:], ALU.add).then_inc(g.kd_ok, 1)
        ve.wait_ge(g.m1_tr, 8)
        own(v.memset(V[:, 0], 0.0))
        for b in range(PAIRS):
            ve.wait_ge(g.v_mm, b + 1)
            src = psC[:, b % 2, :].rearrange("p (r n) -> p n r", r=2)
            own(v.tensor_copy(V[:, 1:NB + 1, :, b], src[:, 0:NB]))
            v.tensor_copy(V[:, NB + 1 + SB:SLOTS, :, b], src[:, NB:NB + SB]).then_inc(g.v_ok, 1)
        own(v.tensor_copy(t2, t1))
        v.tensor_copy(t2, t1).then_inc(g.v_ok, 1)

        for b in range(8):
            ve.wait_ge(g.y1_mm, 2 * b + 2)
            v.tensor_copy(u_s[:, groups(b)].rearrange("p q j c -> p q (j c)"),
                          psB[0:SB, b % 2, :].rearrange("p (q n) -> p q n", q=4)).then_inc(g.y1s_ok, 1)

        ve.wait_ge(g.y1_mm, 16)
        own(v.memset(xpad[:, 0:3], 0.0))
        PER = 23

        def lru(h):
            own(v.tensor_copy(hpar[:, 0:7], lrup[:, bass.ds(h, 1), :].rearrange("p a n -> p (a n)")))
            v.tensor_copy(hpar[:, 7:8], spk[:, bass.ds(h, 1)]).then_inc(g.hcol_ok, 1)
            ve.wait_ge(g.hcol_ok, h + 1)
            own(v.tensor_copy(xpads[:, :, 0:3], cst[:, bass.ds(h, 1)].rearrange("p a b n -> p (a b) n")))
            ve.wait_ge(g.xb_ok, h + 1)
            xcs = xc[:, TP:T].rearrange("p (b l) -> p b l", b=SB)
            own(v.tensor_scalar(xc[:, 0:TP], xpad[:, 0:TP], hpar[:, 0:1], hpar[:, 4:5], ALU.mult, ALU.add))
            own(v.tensor_scalar(xcs, xpads[:, :, 0:SL], hpar[:, 0:1], hpar[:, 4:5], ALU.mult, ALU.add))
            own(v.tensor_copy(nconv[:, bass.ds(h, 1), 0].rearrange("p a n -> p (a n)"), xpad[:, TP:TP + 3]))
            own(v.tensor_copy(nconv[:, bass.ds(h, 1), 1:].rearrange("p a b n -> p (a b) n"), xpads[:, :, SL:SL + 3]))
            for k in range(1, 4):
                own(v.scalar_tensor_tensor(xcs, xpads[:, :, k:k + SL], hpar[:, k:k + 1], xcs, ALU.mult, ALU.add))
                ins = v.scalar_tensor_tensor(xc[:, 0:TP], xpad[:, k:k + TP], hpar[:, k:k + 1], xc[:, 0:TP],
                                             ALU.mult, ALU.add)
                if k < 3:
                    own(ins)
            ins.then_inc(g.conv_ok, 1)
            ve.wait_ge(g.conv_ok, h + 1)
            ve.wait_ge(g.tanh_ok, h + 1)
            own(v.tensor_scalar(dn[:], rt[:], -1.0, 1.0, ALU.mult, ALU.add))
            own(v.reciprocal(dn[:], dn[:]))
            v.scalar_tensor_tensor(av[:], rt[:], 1.0, dn[:], ALU.add, ALU.mult).then_inc(g.den_ok, 1)
            own(v.tensor_tensor(ig[:], ig[:], xc[:], ALU.mult))
            own(v.tensor_tensor(ig[:], ig[:], dn[:], ALU.mult))
            ve.wait_ge(g.den_ok, h + 1)
            ve.wait_ge(g.sqrt_ok, h + 1)
            own(v.tensor_tensor(ig[:], ig[:], rt[:], ALU.mult))
            start_a = av[:, TP:T].rearrange("p (b l) -> p b l", b=SB)[:, :, 0]
            start_b = ig[:, TP:T].rearrange("p (b l) -> p b l", b=SB)[:, :, 0]
            own(v.tensor_tensor(exs[:, 0, 0:SB], start_a, h0[:, bass.ds(h, 1)].rearrange("p a b -> p (a b)"), ALU.mult))
            own(v.tensor_tensor(start_b, start_b, exs[:, 0, 0:SB], ALU.add))
            own(v.memset(start_a, 0.0))
            own(v.tensor_tensor_scan(dn[:], av[:], ig[:], 0.0, ALU.mult, ALU.add))
            own(v.tensor_copy(nlru[:, bass.ds(h, 1), 0:1].rearrange("p a n -> p (a n)"), dn[:, TP - 1:TP]))
            own(v.tensor_copy(nlru[:, bass.ds(h, 1), 1:].rearrange("p a n -> p (a n)"), dn[:, TP + SL - 1:T:SL]))
            ve.wait_ge(g.gb_ok, h + 1)
            own(v.tensor_copy(hpar[:, 7:8], hpar[:, 7:8]))
            v.tensor_tensor(ybT[:, bass.ds(h, 1), :].rearrange("p a n -> p (a n)"), gg[:], dn[:],
                            ALU.mult).then_inc(g.yb_ok, 1)
            ve.wait_ge(g.yb_ok, h + 1)
        with ve.Fori(0, KD - 1) as h:
            own.enter(h * PER)
            lru(h)
        own.leave(KD - 1, PER)
        lru(KD - 1)
        ve.wait_ge(g.sig_ok, 4)
        own(v.tensor_tensor(yaT[:, 0:2], yaT[:, 0:2], sig[:, 0:2], ALU.mult))
        v.tensor_tensor(yaT[:, 2:4], yaT[:, 2:4], sig[:, 2:4], ALU.mult).then_inc(g.ya_done, 1)
        own(v.tensor_copy(hpar[:, 7:8], hpar[:, 7:8]))
        v.tensor_copy(hpar[:, 7:8], hpar[:, 7:8]).then_inc(g.mg_ok, 1)
        with ve.Fori(0, KD) as m:
            ve.wait_ge(g.sga_ok, m + 1)
            ve.wait_ge(g.ya_mm, m + 1)
            for c, (o, n) in enumerate(CHUNKS):
                ins = v.tensor_tensor(mg[:, o:o + n], psB[:, c, 0:n], sga[:, o:o + n], ALU.mult)
            ins.then_inc(g.mga_ok, 1)
            ve.wait_ge(g.sgb_ok, m + 1)
            ve.wait_ge(g.yb_mm, m + 1)
            own.enter(m)
            for c, (o, n) in enumerate(CHUNKS):
                ins = v.tensor_tensor(sgb[:, o:o + n], psB[:, c, 0:n], sgb[:, o:o + n], ALU.mult)
            own(ins)
            ve.wait_ge(g.mga_ok, m + 1)
            v.tensor_tensor(mgT[:, bass.ds(m, 1), :].rearrange("p a n -> p (a n)"), mg[:], sgb[:],
                            ALU.add).then_inc(g.mg_ok, 1)
        own.leave(KD, 1)
        ve.wait_ge(g.gffn_in, 16)
        for t in range(NT):
            n = rows_of(t)
            ps = (psC, psB)[t % 2]
            ve.wait_ge(g.o_mm, t + 1)
            ve.wait_ge(sem(f"xr_in{t % 2}"), 16 * (t // 2 + 1))
            v.tensor_tensor(x2[0:n, t, :], xr[0:n, t % 2, :], ps[0:n, 0:2, :].rearrange("p a n -> p (a n)"),
                            ALU.add).then_inc(g.x2_ok, 1)
            ve.wait_ge(g.ss2_ok, t + 1)
            v.tensor_scalar(rstd2[0:n, t:t + 1], sumsq2[0:n, t:t + 1], 1.0 / D, EPS, ALU.mult,
                            ALU.add).then_inc(g.ms2_ok, 1)
            ve.wait_ge(g.sq2_ok, t + 1)
            own(v.reciprocal(rstd2[0:n, t:t + 1], rstd2[0:n, t:t + 1]))
            v.scalar_tensor_tensor(xn2s[0:n, t % 2, :], x2[0:n, t, :], rstd2[0:n, t:t + 1], gffn[0:n, :],
                                   ALU.mult, ALU.mult).then_inc(g.xn2_ok, 1)
        ve.wait_ge(g.g_sv, 2)
        ve.wait_ge(g.o_mm, NT)
        v.tensor_copy(hpar[:, 7:8], hpar[:, 7:8]).then_inc(g.top_ok, 1)

        def best_keys(h, s, ps=psB):
            ve.wait_ge(g.sc_mm, h * 2 + (s + 1))
            tiles = []
            for t in range(NT):
                n = rows_of(t)
                tiles.append((ps[0:n, t // 4, P * (t % 4):P * (t % 4 + 1)], srep[0:n, t, :],
                              svh[0:n, t, s, 0:8], svh[0:n, t, s, 8:16],
                              sih[0:n, t, s, 0:8], sih[0:n, t, s, 8:16]))
            alone(ve)
            for score, rest, lo, hi, ilo, ihi in tiles:
                ins = v.max(lo, score)
            own(ins)
            alone(ve)
            for score, rest, lo, hi, ilo, ihi in tiles:
                ins = v.match_replace(rest, lo, score, BELOW)
            own(ins)
            alone(ve)
            for score, rest, lo, hi, ilo, ihi in tiles:
                v.max_index(ilo, lo, score)
                ins = v.max(hi, rest)
            own(ins)
            alone(ve)
            for score, rest, lo, hi, ilo, ihi in tiles:
                ins = v.max_index(ihi, hi, rest)
            own(ins)
            v.tensor_copy(exs[:, 0, 0:1], exs[:, 0, 0:1]).then_inc(g.top_ok, 1)

        def keep(h):
            for dst, src in ((sv, svh), (si, sih)):
                view = dst[:, 0:UNITS].rearrange("p (t h) s n -> p t h (s n)", h=HEADS)
                view = view[:, :, bass.ds(h, 1)].rearrange("p t a n -> p t (a n)")
                v.tensor_copy(view[:, 0:NT - 1], src[:, 0:NT - 1].rearrange("p t s n -> p t (s n)"))
                own(v.tensor_copy(view[0:TS, NT - 1:NT], src[0:TS, NT - 1:NT].rearrange("p t s n -> p t (s n)")))
            own(v.tensor_copy(exs[:, 0, 0:1], exs[:, 0, 0:1]))
        with ve.Fori(0, HEADS - 1) as h:
            per = 2 * 4 + 3
            own.enter(h * per)
            best_keys(h, 0)
            best_keys(h, 1)
            keep(h)
        own.leave(HEADS - 1, per)

        own_g = Chain(ve, g.v_g)

        def choose(u, s):
            def half(buf, i):
                return buf[:, bass.ds(u, 1), i].rearrange("p a n -> p (a n)")
            own_g(v.tensor_tensor(cand[:], half(sv, 0).unsqueeze(2).broadcast_to([P, TOPK, TOPK]),
                                  half(sv, 1).unsqueeze(1).broadcast_to([P, TOPK, TOPK]), ALU.add))
            alone(ve)
            own_g(v.max(top[:, 0:8], cand[:]))
            alone(ve)
            own_g(v.match_replace(crep[:], top[:, 0:8], cand[:], BELOW))
            alone(ve)
            own_g(v.max(top[:, 8:16], crep[:]))
            own_g(v.tensor_scalar(gate_sum[:, 0:1], top[:, 0:1], -1.0, None, ALU.mult))
            v.tensor_copy(gate_sum[:, 2:3], top[:, 0:1]).then_inc(g.l2_top, 1)
            cf, rf = cand[:].rearrange("p a b -> p (a b)"), crep[:].rearrange("p a b -> p (a b)")
            v.max_index(pos[:, 0:8], top[:, 0:8], cf)
            own_g(v.max_index(pos[:, 8:16], top[:, 8:16], rf))
            v.tensor_scalar(pab[:, 0], pos[:], 4, None, ALU.logical_shift_right)
            own_g(v.tensor_scalar(pab[:, 1], pos[:], 15, None, ALU.bitwise_and))
            own_g(v.tensor_copy(pabf[:], pab[:]))
            own_g(v.tensor_tensor(hot[:], pabf[:].unsqueeze(3).broadcast_to([P, 2, TOPK, TOPK]),
                                  iota[:].unsqueeze(1).unsqueeze(1).broadcast_to([P, 2, TOPK, TOPK]), ALU.is_equal))
            own_g(v.tensor_tensor(hot[:], hot[:], si[:, bass.ds(u, 1)].rearrange("p a s n -> p (a s) n").unsqueeze(2)
                                  .broadcast_to([P, 2, TOPK, TOPK]), ALU.mult))
            own_g(v.tensor_reduce(pick[:], hot[:], AX.X, ALU.add))
            v.scalar_tensor_tensor(idxu[:, s], pick[:, 0], float(NKEY), pick[:, 1], ALU.mult,
                                   ALU.add).then_inc(g.idx_ok, 1)

        def weigh(u, s):
            ve.wait_ge(g.l2_exp, u + 1)
            own_g(v.reciprocal(gate_sum[:, 2:3], gate_sum[:, 1:2]))
            own_g(v.tensor_scalar(gw[:, s], expt[:], gate_sum[:, 2:3], None, ALU.mult))
            own_g(v.tensor_copy(gate_sum[:, 2:3], gate_sum[:, 1:2]))

        def diagonals(u, s, q, rows):
            ve.wait_ge(g.act_ok, u * 8 + (q + 1))
            for k in (2 * q, 2 * q + 1):
                ve.wait_ge(g.slot_free, u * TOPK + (k + RING - 3))
                v.tensor_scalar(dg[0:rows, k % 4, 0:rows], ident[0:rows, 0:rows], act[0:rows, k:k + 1],
                                gw[0:rows, s, k:k + 1], ALU.mult, ALU.mult).then_inc(g.diag_ok, 1)

        def unit(u, s, rows, between={}):
            for q in range(TOPK // 2):
                for k in (2 * q, 2 * q + 1):
                    r = k % RING
                    ve.wait_ge(gathered[r], u * 32 + 16 * (k // RING + 1))
                    ins = v.tensor_tensor_reduce(ring[0:rows, r, 0:D], ring[0:rows, r, 0:D], xn2c[0:rows, :], 1.0, 0.0,
                                                 ALU.mult, ALU.add, dot[0:rows, k:k + 1])
                ins.then_inc(g.dot_ok, 1)
                if q >= 1:
                    diagonals(u, s, q - 1, rows)
                if q == 0:
                    choose(u + 1, 1 - s)
                if q == 2:
                    weigh(u + 1, 1 - s)
                for step in between.get(q, ()):
                    step()
            diagonals(u, s, TOPK // 2 - 1, rows)

        own_e = Chain(ve, g.v_tail)

        def embedding(t, rows):
            def mean(ready, done):
                def run():
                    ve.wait_ge(ready, t + 1)
                    v.tensor_scalar(tail_s[0:rows, 1:2], tail_s[0:rows, 0:1], 1.0 / D, EPS, ALU.mult,
                                    ALU.add).then_inc(done, 1)
                return run

            def normed():
                ve.wait_ge(g.sq3_ok, t + 1)
                own_e(v.reciprocal(tail_s[0:rows, 2:3], tail_s[0:rows, 1:2]))
                v.tensor_scalar(xn3[0:rows, :], x3[0:rows, :], tail_s[0:rows, 2:3], None, ALU.mult).then_inc(g.xn3_ok, 1)

            def gain():
                ve.wait_ge(g.xn3_tr, t + 1)
                for b in range(2):
                    ins = v.tensor_tensor(xn3T[:, 4 * b:4 * b + 4, 0:rows],
                                          psA[:, b, :].rearrange("p (k n) -> p k n", k=4)[:, :, 0:rows],
                                          gple[:, 4 * b:4 * b + 4].unsqueeze(2).broadcast_to([P, 4, rows]), ALU.mult)
                ins.then_inc(g.xn3T_ok, 1)

            def gated():
                ve.wait_ge(g.gate3_ok, t + 1)
                own_e(v.tensor_tensor(xn3[0:rows, :], xn3[0:rows, :],
                                      psA[0:rows, 0:2, :].rearrange("p a n -> p (a n)"), ALU.mult))
                v.tensor_tensor(x3[0:rows, :], x3[0:rows, :], xn3[0:rows, :], ALU.add).then_inc(g.x4_ok, 1)

            def final():
                ve.wait_ge(g.sq4_ok, t + 1)
                own_e(v.reciprocal(tail_s[0:rows, 2:3], tail_s[0:rows, 1:2]))
                v.scalar_tensor_tensor(xn3[0:rows, :], x3[0:rows, :], tail_s[0:rows, 2:3], gfin[0:rows, :], ALU.mult,
                                       ALU.mult).then_inc(g.y_ok, 1)
            return mean(g.ss3_ok, g.ms3_ok), normed, gain, gated, mean(g.ss4_ok, g.ms4_ok), final

        def tile(t, rows, before, first={}, second={}):
            own_g(v.scalar_tensor_tensor(xn2c[0:rows, :], x2[0:rows, bass.ds(t, 1), :].rearrange("p a n -> p (a n)"),
                                         rstd2[0:rows, bass.ds(t, 1)], gffn[0:rows, :], ALU.mult, ALU.mult))
            if before:
                mean3, normed, gain, gated, mean4, final = embedding(t - 1, P)
                first = {0: [mean3], 2: [normed], 4: [gain]}
                second = {4: [gated], 5: [mean4], 7: [final]}
            unit(t * HEADS, 0, rows, first)
            unit(t * HEADS + 1, 1, rows, second)
            alone(ve)
            with ve.Fori(1, HEADS // 2) as w:
                own_g.enter((w - 1) * (2 * per_unit))
                for s in range(2):
                    unit(t * HEADS + w * 2 + s, s, rows)
            own_g.leave(HEADS // 2 - 1, 2 * per_unit)

        choose(0, 0)
        weigh(0, 0)
        per_unit = own_g.done
        per_tile = 1 + HEADS * per_unit
        ve.wait_ge(g.y_out, 16)
        tile(0, P, False, {3: [lambda: best_keys(HEADS - 1, 0)]},
             {2: [lambda: best_keys(HEADS - 1, 1, psA)], 5: [lambda: keep(HEADS - 1)]})
        with ve.Fori(1, NT - 1) as t:
            own_g.enter((t - 1) * per_tile)
            own_e.enter((t - 1) * 3)
            tile(t, P, True)
        own_g.leave(NT - 2, per_tile)
        own_e.leave(NT - 2, 3)
        tile(NT - 1, TS, True)
        for step in embedding(NT - 1, TS):
            step()

    ctx.close()


_OUT = {
    "o_y": (T, D), "o_s5": (P, 1 + SB, 2, PAIRS), "o_lru": (P, KD, 1 + SB), "o_conv": (P, KD, 1 + SB, 3),
}


def layout(inp):
    import numpy as np
    i = {k: np.asarray(x) for k, x in inp.items()}

    def cols(x):
        return x.reshape(-1, P).T

    def blocks(w):
        k, n = w.shape
        return np.ascontiguousarray(w.reshape(k // P, P, n // P, P).transpose(2, 1, 0, 3))

    def rows(w):
        return np.ascontiguousarray(w.reshape(-1, P, w.shape[1]).transpose(1, 0, 2))

    def state(x):
        x = x.reshape((PAIRS, 2, NS) + x.shape[2:])
        return np.moveaxis(x, 0, 2).reshape((P, PAIRS) + x.shape[3:])

    win = i["w_in"][0]
    o = {}
    o["x"] = np.concatenate([i["x_prompt"][0], i["x_sample"].reshape(TS, D)], axis=0)
    lru = np.stack([cols(i["conv_w"][0, k]) for k in range(4)]
                   + [cols(i[n][0]) for n in ("conv_b", "lru_b_r", "lru_b_i")], axis=2)
    o["par"] = np.concatenate([
        cols(i["g_mix"][0]), cols(i["g_ple"][0]), cols(i["s5_b_glu"][0]), cols(i["lru_lam"][0]),
        lru.reshape(P, -1), i["state_lru"][0].reshape(SB, KD, P).transpose(2, 1, 0).reshape(P, -1),
        i["state_conv"][0].reshape(SB, 3, KD, P).transpose(3, 2, 0, 1).reshape(P, -1)], axis=1)
    ldt = np.broadcast_to(i["s5_log_dt"][0][:, None], (NG, NS))
    o["s5_small"] = np.stack([state(i["s5_lam_re"][0]), state(i["s5_lam_im"][0]), state(ldt)], axis=1)
    o["s5_w"] = np.stack([state(i["s5_b_re"][0]), state(i["s5_b_im"][0]),
                          state(i["s5_c_re"][0].transpose(0, 2, 1)), state(i["s5_c_im"][0].transpose(0, 2, 1))], axis=1)
    o["s5_d"] = i["s5_d"][0]
    h = [np.moveaxis(np.stack([state(x[b]) for b in range(SB)], axis=1), 1, 1)
         for x in (i["state_s5_re"][0], i["state_s5_im"][0])]
    o["h_s5"] = np.stack(h, axis=2)
    o["w_xa"] = rows(win[:, 0:S5W])
    wb = blocks(win[:, S5W:])
    o["w_xb"], o["w_gb"], o["w_ga"], o["w_gp"] = wb[0:8], wb[8:16], wb[16:24], wb[24:32]
    o["w_ri"] = np.stack([i["lru_w_r"][0], i["lru_w_i"][0]], axis=2)
    o["w_glu"] = rows(i["s5_w_glu"][0])
    o["w_ya"], o["w_yb"] = blocks(i["w_a_proj"][0]), blocks(i["w_b_proj"][0])
    o["w_out"] = rows(i["w_out"][0])
    o["g_ffn"], o["g_final"] = i["g_ffn"][0], i["g_final"]
    o["keys"] = i["peer_sub_keys"][0].reshape(2 * HEADS, NKEY, P).transpose(2, 0, 1)
    o["w_q"] = blocks(i["peer_w_q"][0])
    o["uv"] = np.concatenate([i["peer_u"][0], i["peer_v"][0]], axis=1)
    o["w_gate"], o["w_ple"] = rows(i["w_ple_gate"][0]), rows(i["w_ple"][0])
    p = np.concatenate([i["p_prompt"][0, 0], i["p_sample"][0].reshape(TS, -1)], axis=0)
    o["p_T"] = p.T.reshape(2, P, T).transpose(1, 0, 2)
    return {k: np.ascontiguousarray(x) for k, x in o.items()}


def program(nc, arrays):
    a = {n: nc.dram_tensor("in_" + n, x.shape, F32, kind="ExternalInput").ap() for n, x in arrays.items()}
    a.update({n: nc.dram_tensor(n, s, F32, kind="ExternalOutput").ap() for n, s in _OUT.items()})
    a["scr"] = nc.dram_tensor("scr", (TS, S5W), F32).ap()
    build(nc, a)


def kernel(**inputs):
    import numpy as np
    import concourse.bacc as bacc
    from concourse.bass_utils import run_bass_kernel_spmd
    arrays = layout(inputs)
    nc = bacc.Bacc("TRN2", target_bir_lowering=False, num_devices=1)
    program(nc, arrays)
    r = run_bass_kernel_spmd(nc, [{"in_" + n: x for n, x in arrays.items()}], core_ids=[0]).results[0]
    y = np.asarray(r["o_y"])
    s5 = np.asarray(r["o_s5"]).reshape(2, NS, 1 + SB, 2, PAIRS).transpose(3, 2, 4, 0, 1).reshape(2, 1 + SB, NG, NS)
    lru = np.asarray(r["o_lru"]).transpose(2, 1, 0).reshape(1 + SB, D)
    conv = np.asarray(r["o_conv"]).transpose(2, 3, 1, 0).reshape(1 + SB, 3, D)
    c = np.ascontiguousarray
    return (c(y[0:TP].reshape(1, TP, D)), c(y[TP:].reshape(SB, SL, D)),
            c(s5[0, 0:1][None]), c(s5[1, 0:1][None]), c(lru[0:1][None]), c(conv[0:1][None]),
            c(s5[0, 1:][None]), c(s5[1, 1:][None]), c(lru[1:][None]), c(conv[1:][None]))
```
